# Optimizing a Trainium2 kernel written in Bass

```python
import math
import jax, jax.numpy as jnp
from jax import lax
import numpy as np

D_MODEL = 1024
BATCH = 1
SEQ = 128
DEPTH = 2
DEC_BATCH = 1
DEC_SEQ = 256
PAST_LEN = 128

GRID_W = 64
CHUNK = 128
EPS = 1e-6
A_GROUPS = 8
A_GROUP_DIM = 64
A_WIDTH = A_GROUPS * A_GROUP_DIM
B_HEADS = 8
B_QK_DIM = 64
B_V_DIM = 2 * B_QK_DIM
B_QK_WIDTH = B_HEADS * 2 * B_QK_DIM
B_WIDTH = B_HEADS * B_V_DIM
ROPE_THETA = 10000.0
ROPE_AXIS_DIM = B_QK_DIM // 2
ROPE_FREQS = ROPE_AXIS_DIM // 2
C_GROUPS = 4
C_GROUP_DIM = 128
C_WIDTH = C_GROUPS * C_GROUP_DIM
N_BRANCHES = 3
SPLIT_SIZES = (A_WIDTH, A_WIDTH, B_QK_WIDTH, B_QK_WIDTH, B_WIDTH, C_WIDTH, N_BRANCHES * D_MODEL)
IN_COLS = A_WIDTH * 2 + B_QK_WIDTH * 2 + B_WIDTH + C_WIDTH + N_BRANCHES * D_MODEL
N_EXPERTS = 16
N_EXPERT_GROUPS = 4
EXPERTS_PER_GROUP = N_EXPERTS // N_EXPERT_GROUPS
TOP_K = 2
D_EXPERT = 512

kernel_name = "hybrid_flow_prefix_diffattn_gmlp_fnet_moe"

def rms_norm(x, w):
    xf = x.astype(jnp.float32)
    y = xf * lax.rsqrt(jnp.mean(xf * xf, axis=-1, keepdims=True) + EPS)
    return (y * w.astype(jnp.float32)).astype(x.dtype)

def axial_rope_tables(n_tokens):
    grid_rows = n_tokens // GRID_W
    row = jnp.repeat(jnp.arange(grid_rows), GRID_W).astype(jnp.float32)
    col = jnp.tile(jnp.arange(GRID_W), grid_rows).astype(jnp.float32)
    freq = ROPE_THETA ** (-jnp.arange(ROPE_FREQS, dtype=jnp.float32) / ROPE_FREQS)
    ang = jnp.stack([row[:, None] * freq[None, :], col[:, None] * freq[None, :]], axis=1)
    return jnp.cos(ang), jnp.sin(ang)

def apply_axial_rope(x, cos, sin):
    shp = x.shape
    xr = x.astype(jnp.float32).reshape(shp[:-1] + (2, 2, ROPE_FREQS))
    x1, x2 = xr[..., 0, :], xr[..., 1, :]
    cb = cos[None, :, None, None, :, :]
    sb = sin[None, :, None, None, :, :]
    out = jnp.stack([x1 * cb - x2 * sb, x2 * cb + x1 * sb], axis=-2)
    return out.reshape(shp).astype(x.dtype)

def chunk_gmlp(u, v, norm_w, w_s, b_s):
    B, L, _ = u.shape
    u = jax.nn.gelu(u)
    v = rms_norm(jax.nn.gelu(v), norm_w)
    vc = v.reshape(B, L // CHUNK, CHUNK, A_GROUPS, A_GROUP_DIM)
    sv = jnp.einsum('gpq,bnqgc->bnpgc', w_s, vc) + b_s.T[None, None, :, :, None]
    return u * sv.reshape(B, L, A_WIDTH)

def diff_attention(q, k, v, lam):
    B, Lq = q.shape[:2]
    nb = Lq // CHUNK
    scale = 1.0 / math.sqrt(B_QK_DIM)
    qb = q.reshape(B, nb, CHUNK, B_HEADS, 2, B_QK_DIM).transpose(1, 0, 2, 3, 4, 5)
    kf = k.astype(jnp.float32)
    vf = v.astype(jnp.float32)

    def block(qi):
        s = jnp.einsum('bqhmd,bkhmd->bhmqk', qi.astype(jnp.float32), kf) * scale
        p = jax.nn.softmax(s, axis=-1)
        a = p[:, :, 0] - lam * p[:, :, 1]
        return jnp.einsum('bhqk,bkhe->bqhe', a, vf)

    out = lax.map(block, qb)
    return out.transpose(1, 0, 2, 3, 4).reshape(B, Lq, B_HEADS, B_V_DIM).astype(v.dtype)

def fourier_mix(f):
    B, L, _ = f.shape
    ff = f.astype(jnp.float32).reshape(B, L, C_GROUPS, C_GROUP_DIM)
    out = jnp.fft.fft2(ff, axes=(1, 3), norm='ortho').real
    return out.reshape(B, L, C_WIDTH).astype(f.dtype)

def grouped_moe(h, router_w, router_b, w_g, w_u, w_d):
    T = h.shape[0]
    s = jax.nn.sigmoid(jnp.dot(h.astype(jnp.float32), router_w.astype(jnp.float32)))
    sb = (s + router_b.astype(jnp.float32)).reshape(T, N_EXPERT_GROUPS, EXPERTS_PER_GROUP)
    pair, _ = lax.top_k(sb, TOP_K)
    grp = jnp.argmax(pair.sum(-1), axis=-1)
    within = jnp.take_along_axis(sb, grp[:, None, None], axis=1)[:, 0]
    _, local = lax.top_k(within, TOP_K)
    eidx = grp[:, None] * EXPERTS_PER_GROUP + local
    w = jnp.take_along_axis(s, eidx, axis=1)
    w = w / jnp.sum(w, axis=-1, keepdims=True)
    gates = jnp.einsum('tk,tke->te', w, jax.nn.one_hot(eidx, N_EXPERTS, dtype=jnp.float32))
    y = jnp.zeros(h.shape, jnp.float32)
    for e in range(N_EXPERTS):
        a = jax.nn.silu(h @ w_g[e]) * (h @ w_u[e])
        y = y + gates[:, e:e + 1] * (a @ w_d[e]).astype(jnp.float32)
    return y.astype(h.dtype)

def trunk_layer(x, mod, lp, layer_idx, router_w, router_b, rope=None, ctx_k=None, ctx_v=None):
    B, L, D = x.shape
    shift1, scale1, gate1, shift2, scale2, gate2 = jnp.split(mod, 6, axis=-1)
    h = rms_norm(x, lp['norm1_w']) * (1 + scale1) + shift1
    z = h @ lp['w_in']
    u_a, v_a, q, k, v, f_in, g = jnp.split(z, list(np.cumsum(SPLIT_SIZES)[:-1]), axis=-1)
    y_a = chunk_gmlp(u_a, v_a, lp['a_norm_w'], lp['a_w_s'], lp['a_b_s'])
    q = rms_norm(q.reshape(B, L, B_HEADS, 2, B_QK_DIM), lp['q_norm_w'])
    k = rms_norm(k.reshape(B, L, B_HEADS, 2, B_QK_DIM), lp['k_norm_w'])
    v = v.reshape(B, L, B_HEADS, B_V_DIM)
    if rope is not None:
        q = apply_axial_rope(q, *rope)
        k = apply_axial_rope(k, *rope)
    lam_init = 0.8 - 0.6 * math.exp(-0.3 * layer_idx)
    lq = lp['lambda_qk'].astype(jnp.float32)
    lam = jnp.exp(jnp.sum(lq[0] * lq[1])) - jnp.exp(jnp.sum(lq[2] * lq[3])) + lam_init
    if ctx_k is not None:
        keys = jnp.concatenate([ctx_k, k], axis=1)
        vals = jnp.concatenate([ctx_v, v], axis=1)
    else:
        keys, vals = k, v
    o = diff_attention(q, keys, vals, lam)
    o = rms_norm(o, lp['subln_w']) * (1 - lam_init)
    y_b = o.reshape(B, L, B_WIDTH)
    y_c = fourier_mix(f_in)
    gs = jax.nn.sigmoid(g.reshape(B, L, N_BRANCHES, D))
    merged = (gs[:, :, 0] * (y_a @ lp['w_br_a']) + gs[:, :, 1] * (y_b @ lp['w_br_b'])
              + gs[:, :, 2] * (y_c @ lp['w_br_c']))
    x = x + gate1 * (merged @ lp['w_out'])
    h2 = rms_norm(x, lp['norm2_w']) * (1 + scale2) + shift2
    y = grouped_moe(h2.reshape(B * L, D), router_w, router_b, lp['w_e_gate'], lp['w_e_up'], lp['w_e_down'])
    x = x + gate2 * y.reshape(B, L, D)
    return x, k.reshape(B, L, B_HEADS, 2 * B_QK_DIM), v

def setup_inputs(seed: int = 0) -> dict:
    key = jax.random.key(seed)
    ks = iter(jax.random.split(key, 40))
    f32 = jnp.float32

    def nrm(shape, scale=1.0):
        return jax.random.normal(next(ks), shape, f32) * scale

    D = D_MODEL
    return {
        'x_prompt': nrm((BATCH, SEQ, D)),
        'x_sample': nrm((DEC_BATCH, DEC_SEQ, D)),
        'cache_k': nrm((DEC_BATCH, DEPTH, PAST_LEN, B_HEADS, 2 * B_QK_DIM)),
        'cache_v': nrm((DEC_BATCH, DEPTH, PAST_LEN, B_HEADS, B_V_DIM)),
        'c': nrm((DEC_BATCH, D)),
        'c_ctx': nrm((D,)),
        'w_mod': nrm((DEPTH, D, 6 * D), 0.1 * D ** -0.5),
        'b_mod': nrm((DEPTH, 6 * D), 0.02),
        'norm1_w': 1.0 + nrm((DEPTH, D), 0.02),
        'norm2_w': 1.0 + nrm((DEPTH, D), 0.02),
        'w_in': nrm((DEPTH, D, IN_COLS), D ** -0.5),
        'a_norm_w': 1.0 + nrm((DEPTH, A_WIDTH), 0.02),
        'a_w_s': nrm((DEPTH, A_GROUPS, CHUNK, CHUNK), CHUNK ** -0.5),
        'a_b_s': 1.0 + nrm((DEPTH, A_GROUPS, CHUNK), 0.1),
        'q_norm_w': 1.0 + nrm((DEPTH, B_QK_DIM), 0.02),
        'k_norm_w': 1.0 + nrm((DEPTH, B_QK_DIM), 0.02),
        'lambda_qk': nrm((DEPTH, 4, B_QK_DIM), 0.1),
        'subln_w': 1.0 + nrm((DEPTH, B_V_DIM), 0.02),
        'w_br_a': nrm((DEPTH, A_WIDTH, D), A_WIDTH ** -0.5),
        'w_br_b': nrm((DEPTH, B_WIDTH, D), B_WIDTH ** -0.5),
        'w_br_c': nrm((DEPTH, C_WIDTH, D), C_WIDTH ** -0.5),
        'w_out': nrm((DEPTH, D, D), D ** -0.5),
        'router_w': nrm((D, N_EXPERTS), D ** -0.5),
        'router_b': nrm((N_EXPERTS,), 0.01),
        'w_e_gate': nrm((DEPTH, N_EXPERTS, D, D_EXPERT), D ** -0.5),
        'w_e_up': nrm((DEPTH, N_EXPERTS, D, D_EXPERT), D ** -0.5),
        'w_e_down': nrm((DEPTH, N_EXPERTS, D_EXPERT, D), D_EXPERT ** -0.5),
    }

def reference(x_prompt, x_sample, cache_k, cache_v, c, c_ctx, w_mod, b_mod, norm1_w, norm2_w,
              w_in, a_norm_w, a_w_s, a_b_s, q_norm_w, k_norm_w, lambda_qk, subln_w,
              w_br_a, w_br_b, w_br_c, w_out, router_w, router_b, w_e_gate, w_e_up, w_e_down):
    rope = axial_rope_tables(x_sample.shape[1])
    xp, xs = x_prompt, x_sample
    new_k, new_v = [], []
    for l in range(DEPTH):
        lp = dict(norm1_w=norm1_w[l], norm2_w=norm2_w[l], w_in=w_in[l], a_norm_w=a_norm_w[l],
                  a_w_s=a_w_s[l], a_b_s=a_b_s[l], q_norm_w=q_norm_w[l], k_norm_w=k_norm_w[l],
                  lambda_qk=lambda_qk[l], subln_w=subln_w[l], w_br_a=w_br_a[l], w_br_b=w_br_b[l],
                  w_br_c=w_br_c[l], w_out=w_out[l], w_e_gate=w_e_gate[l], w_e_up=w_e_up[l],
                  w_e_down=w_e_down[l])
        mod_ctx = (jax.nn.silu(c_ctx) @ w_mod[l] + b_mod[l])[None, None, :]
        mod_lat = (jax.nn.silu(c) @ w_mod[l] + b_mod[l])[:, None, :]
        xp, k_l, v_l = trunk_layer(xp, mod_ctx, lp, l, router_w, router_b)
        new_k.append(k_l)
        new_v.append(v_l)
        ck = cache_k[:, l].reshape(cache_k.shape[0], cache_k.shape[2], B_HEADS, 2, B_QK_DIM)
        cv = cache_v[:, l]
        xs, _, _ = trunk_layer(xs, mod_lat, lp, l, router_w, router_b, rope=rope, ctx_k=ck, ctx_v=cv)
    new_k_arr = jnp.stack(new_k, axis=1)
    new_v_arr = jnp.stack(new_v, axis=1)
    return (xp, xs, new_k_arr, new_v_arr)


_drawn_inputs = setup_inputs


def setup_inputs(seed=0):
    import zlib

    import numpy as np

    out = dict(_drawn_inputs(seed))
    spreads = {}
    factors = {'cache_k': 3.346,
     'cache_v': 2.938,
     'norm1_w': 2.834,
     'norm2_w': 8.0,
     'a_norm_w': 8.0,
     'a_b_s': 8.0,
     'q_norm_w': 8.0,
     'k_norm_w': 2.8,
     'lambda_qk': 8.0,
     'subln_w': 8.0,
     'router_b': 6.254}
    for name, (base, spread) in spreads.items():
        noise = np.random.default_rng([zlib.crc32(name.encode()), seed]).standard_normal(out[name].shape)
        drawn = base * np.exp(spread * noise) if base else spread * noise
        out[name] = __import__('jax').numpy.asarray(drawn.astype(out[name].dtype))
    for name, factor in factors.items():
        out[name] = (out[name] * factor).astype(out[name].dtype)
    return out
```

```python
import math

import concourse.bass as bass
from concourse import mybir

F32 = mybir.dt.float32
F32R = mybir.dt.float32r
I32 = mybir.dt.int32
ACT = mybir.ActivationFunctionType
ALU = mybir.AluOpType
AX = mybir.AxisListType

P = 128
DEPTH = 2
D = 1024
NT = 3
T = NT * P
KD = D // P
W = 512
IN_COLS = 7680
HEADS = 8
MAPS = 2
DQ = 64
EPS = 1e-6
NE = 16
EG = 4
RAW = 3
RING = 3
RING_MOE = 6
LAM_INIT = [0.8 - 0.6 * math.exp(-0.3 * l) for l in range(DEPTH)]

MOD_BLOCKS = 12
PAIRS_MOD = 4 * MOD_BLOCKS
W_IN_ORDER = [0, 1, 8, 2, 3, 4, 5, 6, 7]
BRANCHES = [("a", 0, 4), ("c", 2, 4), ("b", 1, 8)]
PAIRS_W_IN = 4 * len(W_IN_ORDER)
PAIRS_BR = sum(2 * (4 + s // 2) for _, _, s in BRANCHES)
PAIRS_OUT = 8
PAIRS_DENSE = PAIRS_W_IN + PAIRS_BR + PAIRS_OUT
PAIRS_EXPERT = 12
PAIRS_MOE = PAIRS_EXPERT * NE
PAIRS = PAIRS_MOD + PAIRS_DENSE + PAIRS_MOE
POOL_Q = (2, 3, 8, 9)
PAIRS_POOL = PAIRS_DENSE + len(POOL_Q) * NE
PAIRS_DVE = PAIRS - PAIRS_POOL
CHUNKS = PAIRS // 2
assert PAIRS % RING == 0 and CHUNKS % RAW == 0 and PAIRS_EXPERT % RING_MOE == 0
assert (PAIRS_MOD + PAIRS_DENSE) % RING_MOE == 0 and (PAIRS_EXPERT // 2) % RAW == 0

USES = [("in", b, 0, 4) for b in W_IN_ORDER]
for _name, _g, _s in BRANCHES:
    for _h in range(2):
        USES.append(("gate", _g, _h, 4))
        USES.append(("br", _name, _h, _s // 2))
USES += [("out", 0, h, 4) for h in range(2)]
N_IN = len(W_IN_ORDER)
FIRST_BR = N_IN
ATT_PAIRS = 24

R_NORM1 = 0
R_WS = R_NORM1 + KD
R_SV = R_WS + 2
R_YA = R_SV + 4
R_DFT = R_YA + 4
AUX = R_DFT + 12
R_YB = AUX
R_MERGED = R_YB + HEADS
R_NORM2 = R_MERGED + KD
R_BACK = R_NORM2 + KD
R_LOGITS = R_BACK + 4 * NT
R_SLOTS = R_LOGITS + 1
AUX_ROUNDS = R_SLOTS + 1

PER = dict(
    pair_used=PAIRS, hi_done=PAIRS, lo_dve=PAIRS_DVE, lo_pool=PAIRS_POOL,
    mod_acc=MOD_BLOCKS, modrow_done=MOD_BLOCKS, mcol_acc=1, col_ready=1, gate_acc=8, gate_done=8,
    sumsq=2, meansq=2, root=2, xn_done=2, full_done=2 * KD, hT_hi=2 * KD, hT_ready=2 * KD,
    aux_ready=AUX_ROUNDS, aux_free=AUX_ROUNDS,
    acc_ready=len(USES), evac_act=N_IN + 6, evac_dve=8,
    v_sumsq=1, v_meansq=1, v_root=1, vn_done=1, ya_tok=1, ya_hi=4, ya_ready=4,
    yc_hi=4, yc_ready=4, dft_copied=4,
    qk_sumsq=6, qk_meansq=1, qk_root=1, qk_normed=1, rope_ready=1,
    lam_exp=1, lam_dot=1, lam_ready=1,
    qkT_acc=HEADS, qT_done=HEADS, kT_done=HEADS, score_acc=2 * HEADS, score_max=3 * HEADS,
    exp_done=3 * HEADS, diff_done=3 * HEADS, aT_acc=2 * HEADS, aT_copied=2 * HEADS,
    o_acc=HEADS, o_copied=HEADS, o_sumsq=1, o_meansq=1, o_root=1, o_normed=1,
    yb_hi=HEADS, yb_ready=HEADS, merged_done=6, mT_hi=KD, mT_ready=KD, x_mid=1,
    h2h_done=2 * NT, h2_ready=1, score_done=1, mask_done=1, slot_done=1, flag_ready=1,
    pick_ready=NE, X_acc=NE, PT_acc=NE, PT_done=NE, xe_hi=NE, xe_ready=NE, silu_done=NE,
    a_done=NE, eT_acc=NE, eT_hi=NE, eT_ready=NE, out_hi=NE, out_ready=NE,
    comb_acc=6 * NE, comb_done=6 * NE, y_zero=1, x_ready=1,
    small_in=16 * 9, cache_in=16 * 2, kv_out=16 * 2, dft_in=16 * 3,
)
CREDIT = dict(pair_used=RING, x_ready=1)


OVER_PE = dict(gathered=1, c0=2, c1=3, c2=4, c3=5, turned=6, c4=7, c5=8, part=9)
OVER_ACT = dict(x_hi=1, c0=2, c1=3, c2=4, c3=5, silu=6, a_hi=7, c4=8, c5=9, out_hi=10)
OVER_DVE = dict(pick=1, x_lo=2, pickT=3, c0=4, c1=5, c2=6, c3=7, a=8, a_lo=9, c4=10, c5=11, out_lo=12, part=13)
OVER_STEPS = dict(pe=14, act=10, dve=18, dma=16 * 6)
SLOT_BASE = 0


def build(nc, io):
    sems = {}

    def sem(name):
        if name not in sems:
            sems[name] = nc.alloc_semaphore(name)
        return sems[name]

    def at(name, l, k):
        return l * PER[name] + CREDIT.get(name, 0) + k

    top = [(nc.sbuf_base + 63) // 64 * 64]

    def place(name, shape, dt, offset=None):
        size = 4 * math.prod(shape[1:])
        if offset is None:
            offset = top[0]
            top[0] += (size + 31) // 32 * 32
        return nc.alloc_sbuf_tensor_at(name, shape, dt, offset=offset)

    def room(size):
        offset = top[0]
        top[0] += size
        return offset

    x = place("x", [P, NT, D], F32)
    raw = place("raw", [P, RAW, 4, W], F32)
    wh_at = top[0]
    wh = place("wh", [P, RING, 2, W], F32R)
    hTh = place("hTh", [P, KD, T], F32R)
    wl_at = top[0]
    wl = place("wl", [P, RING, 2, W], F32R)
    hTl = place("hTl", [P, KD, T], F32R)
    assert 4 * KD * T == 4 * (RING_MOE - RING) * 2 * W
    wxh = place("wxh", [P, RING_MOE, 2, W], F32R, wh_at)
    wxl = place("wxl", [P, RING_MOE, 2, W], F32R, wl_at)
    gbc = place("gbc", [P, 2, 2, D], F32)
    r_uv, r_qk, r_vv, r_f = room(12288), room(24576), room(12288), room(6144)
    r_ya, r_yc, r_kc, r_z = room(12288), room(12288), room(8192), room(14336)
    uv = place("uv", [P, NT, 2 * W], F32, r_uv)
    merged = place("merged", [P, NT, D], F32, r_uv)
    xn = place("xn", [P, NT, D], F32, r_uv)
    qk = place("qk", [P, HEADS, 2, NT, P], F32, r_qk)
    ybT = place("ybT", [P, HEADS, 2, T], F32R, r_qk)
    modrow = place("modrow", [5, MOD_BLOCKS, W], F32, r_qk)
    vv = place("vv", [P, NT, D], F32, r_vv)
    f_in = place("f_in", [P, NT, W], F32, r_f)
    gs = place("gs", [P, NT, W], F32, r_f)
    yaT = place("yaT", [P, 2, 4, T], F32R, r_ya)
    ycT = place("ycT", [P, 2, 4, T], F32R, r_yc)
    mT = place("mT", [P, 2, KD, T], F32R, r_ya)
    junk = place("junk", [P, D], F32, r_yc)
    full = place("full", [P, 2, T], F32, r_yc + 4096)
    qsq = place("qsq", [P, D], F32, r_f)
    kc = place("kc", [P, HEADS, P], F32, r_kc)
    vc = place("vc", [P, HEADS, P], F32, r_kc + 4096)
    dft_lat = place("dft_lat", [P, 2, 2, 256], F32, r_kc)
    dft_pr = place("dft_pr", [P, 2, P], F32, r_kc + 4096)
    dft_ch = place("dft_ch", [P, 2, P], F32, r_kc + 5120)
    ws = place("ws", [P, 8, P], F32, r_z)
    wsT = place("wsT", [P, 8, P], F32, r_z + 4096)
    spec = place("spec", [P, 2, T], F32, r_z)
    anorm = place("anorm", [P, W], F32, r_z + 8192)
    rope = place("rope", [P, 2, 2, 2, P], F32, r_z + 10240)
    qT = place("qT", [P, T], F32, r_z)
    kT = place("kT", [P, 4 * P], F32, r_z + 1536)
    e0 = place("e0", [P, MAPS, P], F32, r_z + 3584)
    e12 = place("e12", [P, 2, MAPS, T], F32, r_z + 4608)
    aT = place("aT", [P, 7, P], F32, r_z + 10752)
    xeT = place("xeT", [P, 2, KD, P], F32R, r_uv)
    eaT = place("eaT", [P, 2, 4, P], F32R, r_uv + 8192)
    h2 = place("h2", [P, 2, NT, D], F32R, r_qk)
    y = place("y", [P, NT, D], F32, r_vv)
    pick = place("pick", [P, NT, P], F32R, r_f)
    pickT = place("pickT", [P, 2, NT, P], F32R, r_f + 1536)
    oe = place("oe", [P, 2, D], F32R, r_ya)
    sg = place("sg", [P, W], F32, r_kc)
    ae = place("ae", [P, W], F32, r_kc + 2048)
    rt = place("rt", [P, 8, 192], F32, r_z)

    ident = place("ident", [P, P], F32)
    tri = place("tri", [P, 2, P], F32)
    iota = place("iota", [P, P], F32)
    rank_tri = place("rank_tri", [P, EG, EG], F32)
    sel2 = place("sel2", [5, 2], F32)
    selb = place("selb", [5, 2, P], F32)
    rope0 = place("rope0", [P, 2, 2, P], F32, r_yc + 9216)
    crow = place("crow", [16, P], F32, r_yc + 7168)
    csil = place("csil", [P, 16], F32)
    cs = place("cs", [P, KD, 4], F32R)
    rw = place("rw", [P, KD, NE], F32, r_yc + 7680)
    rwh = place("rwh", [P, KD, NE], F32R)
    rwl = place("rwl", [P, KD, NE], F32R)
    rb = place("rb", [P, NE], F32)
    srow = place("srow", [25, P], F32, r_yc + 11264)
    scol = place("scol", [P, 25], F32)
    qkn = place("qkn", [P, 2, MAPS, DQ], F32)
    lamv = place("lamv", [P, 4, DQ], F32, r_yc + 8192)
    laminit = place("laminit", [P, DEPTH, 2], F32)
    lam = place("lam", [P, 8], F32)
    scl = place("scl", [P, 2, KD, 2], F32)
    shf = place("shf", [P, 2, KD, 2], F32)
    st = place("st", [P, 16], F32)
    qst = place("qst", [P, 6, 16], F32)
    mx = place("mx", [P, 3, MAPS], F32)
    nmx = place("nmx", [P, 3, MAPS], F32)
    es = place("es", [P, 3, MAPS], F32)
    er = place("er", [P, 3, MAPS], F32)
    subc = place("subc", [P, 1], F32)
    s_r = place("s_r", [P, NT, NE], F32)
    slot = place("slot", [P, NT, NE], F32)
    mask = place("mask", [P, NT, NE], F32)
    gate = place("gate", [P, NT, NE], F32)
    cnt = place("cnt", [P, 8], F32)
    flag = place("flag", [P, 2], I32)
    assert top[0] <= nc.sbuf_usable_end, (top[0], nc.sbuf_usable_end)

    ps = nc.alloc_psum_tensor("ps", [P, 8, W], F32)

    w_mod = io["w_mod"].rearrange("l k n -> (l k) n")
    w_in = io["w_in"].rearrange("l k n -> (l k) n")
    w_out = io["w_out"].rearrange("l k n -> (l k) n")
    w_br = {b: io["w_br_" + b].rearrange("l k n -> (l k) n") for b in "abc"}
    w_eg = io["w_e_gate"].rearrange("l e k n -> (l e k) n")
    w_eu = io["w_e_up"].rearrange("l e k n -> (l e k) n")
    w_ed = io["w_e_down"].rearrange("l e k n -> (l e k) n")

    class Chain:

        def __init__(self, eng, name):
            self.eng, self.sem, self.n = eng, nc.alloc_semaphore(name), 0

        def link(self, ins):
            self.n += 1
            ins.then_inc(self.sem, 1)
            self.eng.wait_ge(self.sem, self.n)

    def over_at(eng, e, b, k):
        return e * (2 * OVER_STEPS[eng]) + ((b - 1) * OVER_STEPS[eng] + k)

    def second_pass(eng, l, turn):
        eng.wait_ge(sem("flag_ready"), at("flag_ready", l, 1))
        over = eng.value_load(flag[0:1, 0:1], min_val=0, max_val=1)
        with eng.If(over > 0):
            with eng.Fori(0, NE) as e:
                for b in (1, 2):
                    turn(e, b)
            eng.wait_ge(sem(f"over_dve{l}"), 2 * NE * OVER_STEPS["dve"])
        eng.end_ifs()

    def expert_loop(eng, expert):
        expert(0, 0, first=True)
        with eng.Fori(0, (NE - 2) // 2) as i:
            expert(i * 2 + 1, 1)
            expert(i * 2 + 2, 0)
        expert(NE - 1, (NE - 1) % 2, last_one=True)

    landed = [sem(f"chunk_landed{i}") for i in range(RAW)]

    def chunk_at(l, c):
        return 16 * (l * (CHUNKS // RAW) + c // RAW + 1)

    CHUNKS_EXPERT = PAIRS_EXPERT // 2

    def pairs_by(l, e, q, pairs_kept):
        kept = [i for i in range(PAIRS_EXPERT) if pairs_kept(i)]
        return len(kept) * (e + q // PAIRS_EXPERT) + sum(1 for i in kept if i <= q % PAIRS_EXPERT)

    def used_at(l, e, q):
        return at("pair_used", l, PAIRS_MOD + PAIRS_DENSE + q + 1) + e * PAIRS_EXPERT

    def lo_at(l, e, q):
        pool = q % PAIRS_EXPERT in POOL_Q
        n = pairs_by(l, e, q, lambda i: (i in POOL_Q) == pool)
        return ("lo_pool", at("lo_pool", l, PAIRS_DENSE) + n) if pool else ("lo_dve", at("lo_dve", l, PAIRS_MOD) + n)

    def expert_chunk_at(l, e, j):
        return 16 * (l * (CHUNKS // RAW) + (PAIRS_MOD + PAIRS_DENSE) // 2 // RAW + j // RAW + 1) + e * (16 * (CHUNKS_EXPERT // RAW))

    def sync_program(sp):
        def split(l, e, j):
            name, value = lo_at(l, e, 2 * j + 1)
            sp.wait_ge(sem(name), value)

        def load(l, c, src, row, col):
            p = 2 * (c - RAW) + 2
            if c < RAW:
                if l > 0:
                    split(l - 1, NE - 1, CHUNKS_EXPERT + c - RAW)
            elif p <= PAIRS_MOD:
                sp.wait_ge(sem("lo_dve"), at("lo_dve", l, p))
            else:
                sp.wait_ge(sem("lo_pool"), at("lo_pool", l, p - PAIRS_MOD))
            sp.dma_start(raw[:, c % RAW, :, :],
                         src[bass.ds(row, 4 * P), col:col + W].rearrange("(k p) n -> p k n", p=P)
                         ).then_inc(landed[c % RAW], 16)

        for t in range(NT):
            src = io["x_prompt"][0, :, :] if t == 0 else io["x_sample"][0, (t - 1) * P:t * P, :]
            sp.dma_start(x[:, t, :], src).then_inc(sem("x_in"), 16)
        for l in range(DEPTH):
            c = 0
            for n in range(MOD_BLOCKS):
                for k in range(2):
                    load(l, c, w_mod, l * D + k * W, n * W)
                    c += 1
            for kind, which, half, pairs in USES:
                for k in range(pairs // 2):
                    if kind == "in":
                        load(l, c, w_in, l * D + k * W, which * W)
                    elif kind == "gate":
                        load(l, c, w_in, l * D + k * W, IN_COLS - 3 * D + which * D + half * W)
                    elif kind == "br":
                        load(l, c, w_br[which], l * pairs * 2 * P + k * W, half * W)
                    else:
                        load(l, c, w_out, l * D + k * W, half * W)
                    c += 1
            def expert(e, odd, first=False, last_one=False):
                for j in range(CHUNKS_EXPERT):
                    if first and j < RAW:
                        sp.wait_ge(sem("lo_pool"), at("lo_pool", l, PAIRS_DENSE + 2 * (j - RAW) + 2))
                    else:
                        split(l, e, j - RAW)
                    if j < 4:
                        src, row, col = (w_eg, w_eu)[j // 2], (l * NE + e) * D + j % 2 * W, 0
                    else:
                        src, row, col = w_ed, (l * NE + e) * W, (j - 4) * W
                    sp.dma_start(raw[:, j % RAW, :, :],
                                 src[bass.ds(row, 4 * P), col:col + W].rearrange("(k p) n -> p k n", p=P)
                                 ).then_inc(landed[j % RAW], 16)

            expert_loop(sp, expert)

            def turn(e, b):
                for i in range(6):
                    sp.wait_ge(sem(f"over_dve{l}"), over_at("dve", e, b, OVER_DVE["pick"] if i == 0 else OVER_DVE[f"c{i - 1}"]))
                    src = (w_eg, w_eg, w_eu, w_eu, w_ed, w_ed)[i]
                    row = (l * NE + e) * (D if i < 4 else W) + (i % 2 * W if i < 4 else 0)
                    col = 0 if i < 4 else (i % 2) * W
                    sp.dma_start(raw[:, 0, :, :], src[bass.ds(row, 4 * P), col:col + W].rearrange("(k p) n -> p k n", p=P)
                                 ).then_inc(sem(f"over_dma{l}"), 16)

            second_pass(sp, l, turn)
        sp.wait_ge(sem("x_ready"), at("x_ready", DEPTH - 1, 1))
        for t in range(NT):
            dst = io["y_prompt"][0, :, :] if t == 0 else io["y_sample"][0, (t - 1) * P:t * P, :]
            sp.dma_start(dst, x[:, t, :]).then_inc(sem("y_out"), 16)
        sp.wait_ge(sem("y_out"), 16 * NT)

    def tensor_program(pe):
        T3 = ((0, 0), (0, 1), (1, 0))

        def mm3(out, act_hl, w_hl, start, stop):
            for n, (i, j) in enumerate(T3):
                ins = pe.matmul(out, act_hl[i], w_hl[j], start=start and n == 0, stop=stop and n == 2)
            return ins

        def wait_pair(l, p):
            if p < PAIRS_MOD:
                pe.wait_ge(sem("lo_dve"), at("lo_dve", l, p + 1))
            else:
                pe.wait_ge(sem("lo_pool"), at("lo_pool", l, p - PAIRS_MOD + 1))

        def transpose(out, in_, **kw):
            n = in_.shape[0]
            return pe.transpose(out, in_, ident[0:n, 0:n])

        pe.wait_ge(sem("const_in"), 16 * N_CONST)
        transpose(ps[:, 0, 0:16], crow[:, :]).then_inc(sem("crow_acc"), 1)
        pe.sem_inc(sem("pair_used"), CREDIT["pair_used"])
        pe.wait_ge(sem("cs_ready"), 2)

        for l in range(DEPTH):
            for n in range(MOD_BLOCKS):
                if n >= 2:
                    pe.wait_ge(sem("modrow_done"), at("modrow_done", l, n - 1))
                elif l > 0:
                    pe.wait_ge(sem("comb_done"), at("comb_done", l - 1, 6 * NE))
                for q in range(4):
                    p = 4 * n + q
                    wait_pair(l, p)
                    for i in range(2):
                        k = 2 * q + i
                        for w in (wh, wl):
                            last = pe.matmul(ps[0:4, n % 2, :], cs[:, k, :], w[:, p % RING, i, :],
                                             start=k == 0 and w is wh, stop=k == KD - 1 and w is wl)
                    last.then_inc(sem("pair_used"), 1)
                pe.matmul(ps[0:1, 7, 0:2], sel2[:, 0:1], sel2[:, :], start=True, stop=True
                          ).then_inc(sem("mod_acc"), 1)
            pe.wait_ge(sem("small_in"), at("small_in", l, 16 * 9))
            transpose(ps[:, 2, 64:89], srow[:, :])
            pe.wait_ge(sem("modrow_done"), at("modrow_done", l, MOD_BLOCKS))
            for i, n in enumerate((0, 1, 2, 3, 6, 7, 8, 9)):
                for k in range(4):
                    o = 8 * i + 2 * k
                    last = pe.matmul(ps[:, 2, o:o + 2], modrow[:, n, k * P:(k + 1) * P], sel2[:, :],
                                     start=True, stop=True)
            last.then_inc(sem("mcol_acc"), 1)
            i = 0
            for n in (4, 5, 10, 11):
                for g in range(2):
                    if i >= 2:
                        pe.wait_ge(sem("gate_done"), at("gate_done", l, i - 1))
                    pe.matmul(ps[:, 3 + i % 2, :], selb[:, g, :], modrow[:, n, :], start=True, stop=True
                              ).then_inc(sem("gate_acc"), 1)
                    i += 1

            def aux_start(r):
                if r >= 2:
                    pe.wait_ge(sem("aux_free"), at("aux_free", l, r - 1))
                return ps[:, 6 + r % 2, :]

            def norm_transposes(which, r0):
                for k in range(KD):
                    out = aux_start(r0 + k)
                    if k == 0:
                        pe.wait_ge(sem("xn_done"), at("xn_done", l, which + 1))
                    for t in range(NT):
                        last = transpose(out[:, t * P:(t + 1) * P], xn[:, t, k * P:(k + 1) * P])
                    last.then_inc(sem("aux_ready"), 1)

            norm_transposes(0, R_NORM1)
            pe.wait_ge(sem("gate_done"), at("gate_done", l, 8))
            pe.wait_ge(sem("col_ready"), at("col_ready", l, 1))

            def act_done(u):
                return sum(1 for k in USES[:u] if k[0] in ("in", "gate"))

            def dense():
                p = PAIRS_MOD
                for u, (kind, which, half, pairs) in enumerate(USES):
                    beside = FIRST_BR <= u < FIRST_BR + 8
                    base = 0 if beside else 3 * (u % 2)
                    prev = u - 1 if beside else u - 2
                    if prev >= 0:
                        if USES[prev][0] in ("in", "gate"):
                            pe.wait_ge(sem("evac_act"), at("evac_act", l, act_done(prev + 1)))
                        else:
                            pe.wait_ge(sem("evac_dve"), at("evac_dve", l, prev + 1 - act_done(prev + 1)))
                    if u == FIRST_BR + 8:
                        pe.wait_ge(sem("o_copied"), at("o_copied", l, HEADS))
                    for q in range(pairs):
                        wait_pair(l, p)
                        for i in range(2):
                            k = 2 * q + i
                            if kind in ("in", "gate"):
                                if u == 0:
                                    pe.wait_ge(sem("hT_ready"), at("hT_ready", l, k + 1))
                                hl = (hTh[:, k, :], hTl[:, k, :])
                            elif kind == "out":
                                if half == 0:
                                    pe.wait_ge(sem("mT_ready"), at("mT_ready", l, k + 1))
                                hl = (mT[:, 0, k, :], mT[:, 1, k, :])
                            elif which == "a":
                                hl = (yaT[:, 0, k, :], yaT[:, 1, k, :])
                            elif which == "c":
                                hl = (ycT[:, 0, k, :], ycT[:, 1, k, :])
                            else:
                                if half == 0:
                                    pe.wait_ge(sem("yb_ready"), at("yb_ready", l, k + 1))
                                hl = (ybT[:, k, 0, :], ybT[:, k, 1, :])
                            if which == "a" and half == 0 and kind == "br" and k == 0:
                                pe.wait_ge(sem("ya_ready"), at("ya_ready", l, 4))
                            if which == "c" and half == 0 and kind == "br" and k == 0:
                                pe.wait_ge(sem("yc_ready"), at("yc_ready", l, 4))
                            for t in range(NT):
                                c = slice(t * P, (t + 1) * P)
                                last = mm3(ps[:, base + t, :], (hl[0][:, c], hl[1][:, c]),
                                           (wh[:, p % RING, i, :], wl[:, p % RING, i, :]),
                                           start=k == 0, stop=k == 2 * pairs - 1)
                        if q == pairs - 1:
                            last.then_inc(sem("acc_ready"), 1)
                            pe.wait_ge(sem("acc_ready"), at("acc_ready", l, u + 1))
                            pe.sem_inc(sem("pair_used"), 1)
                        else:
                            last.then_inc(sem("pair_used"), 1)
                        p += 1
                        yield

            stream = dense()

            def pump(n):
                for _ in range(n):
                    next(stream)

            pump(4 * 4)
            for i in range(2):
                out = aux_start(R_WS + i)
                for g in range(4):
                    last = transpose(out[:, g * P:(g + 1) * P], ws[:, 4 * i + g, :])
                last.then_inc(sem("aux_ready"), 1)
            pump(2)
            for i in range(4):
                out = aux_start(R_SV + i)
                if i == 0:
                    pe.wait_ge(sem("vn_done"), at("vn_done", l, 1))
                for j in range(2):
                    g = 2 * i + j
                    last = pe.matmul(out[:, j * 192:(j + 1) * 192].rearrange("p (t c) -> p t c", t=NT),
                                     wsT[:, g, :], uv[:, :, W + g * 64:W + (g + 1) * 64],
                                     start=True, stop=True)
                last.then_inc(sem("aux_ready"), 1)
            pump(2)
            for i in range(4):
                out = aux_start(R_YA + i)
                if i == 0:
                    pe.wait_ge(sem("ya_tok"), at("ya_tok", l, 1))
                for t in range(NT):
                    last = transpose(out[:, t * P:(t + 1) * P], uv[:, t, i * P:(i + 1) * P])
                last.then_inc(sem("aux_ready"), 1)
            pump(2)
            pe.wait_ge(sem("dft_in"), at("dft_in", l, 48))
            for g in range(4):
                c = slice(g * P, (g + 1) * P)
                out = aux_start(R_DFT + 3 * g)
                for t in range(2):
                    last = pe.matmul(out, f_in[:, 1 + t, c], dft_lat[:, t, :, :].rearrange("p s n -> p (s n)"),
                                     start=t == 0, stop=t == 1)
                last.then_inc(sem("aux_ready"), 1)
                out = aux_start(R_DFT + 3 * g + 1)
                pe.matmul(out[:, 0:256], f_in[:, 0, c], dft_pr[:, :, :].rearrange("p s n -> p (s n)"),
                          start=True, stop=True).then_inc(sem("aux_ready"), 1)
                pump(1)
                out = aux_start(R_DFT + 3 * g + 2)
                pe.wait_ge(sem("dft_copied"), at("dft_copied", l, g + 1))
                for s in range(2):
                    last = pe.matmul(out[:, 0:T], dft_ch[:, s, :], spec[:, s, :], start=s == 0, stop=s == 1)
                last.then_inc(sem("aux_ready"), 1)
            pump(PAIRS_W_IN - 4 * 4 - 6 - 4)

            pe.wait_ge(sem("evac_act"), at("evac_act", l, N_IN))
            pe.wait_ge(sem("aux_free"), at("aux_free", l, AUX))
            pe.wait_ge(sem("cache_in"), at("cache_in", l, 32))
            pe.wait_ge(sem("qk_normed"), at("qk_normed", l, 1))
            for h in range(HEADS):
                if h:
                    pe.wait_ge(sem("exp_done"), at("exp_done", l, 3 * h))
                for t in range(NT):
                    transpose(ps[:, 6, t * P:(t + 1) * P], qk[:, h, 0, t, :])
                transpose(ps[:, 7, 0:P], kc[:, h, :])
                for t in range(NT):
                    last = transpose(ps[:, 7, (3 if t == 0 else t) * P:(4 if t == 0 else t + 1) * P],
                                     qk[:, h, 1, t, :])
                last.then_inc(sem("qkT_acc"), 1)
                pump(1)
                pe.wait_ge(sem("qT_done"), at("qT_done", l, h + 1))
                pe.wait_ge(sem("kT_done"), at("kT_done", l, h + 1))
                if h:
                    pe.wait_ge(sem("o_copied"), at("o_copied", l, h))
                for t in (1, 0, 2):
                    for m in range(MAPS):
                        rows = slice(m * DQ, (m + 1) * DQ)
                        if t == 0:
                            out, keys = ps[:, 4 + m, T:4 * P], kT[rows, 3 * P:4 * P]
                        else:
                            out, keys = ps[:, (4 if t == 1 else 6) + m, 0:T], kT[rows, 0:T]
                        last = pe.matmul(out, qT[rows, t * P:(t + 1) * P], keys, start=True, stop=True)
                    if t != 1:
                        last.then_inc(sem("score_acc"), 1)
                pump(1)
                pe.wait_ge(sem("diff_done"), at("diff_done", l, 3 * h + 2))
                for j in range(3):
                    transpose(ps[:, 3, j * P:(j + 1) * P], e12[:, 0, 0, j * P:(j + 1) * P])
                transpose(ps[:, 3, 3 * P:4 * P], e0[:, 0, :]).then_inc(sem("aT_acc"), 1)
                pe.wait_ge(sem("diff_done"), at("diff_done", l, 3 * h + 3))
                for j in range(3):
                    last = transpose(ps[:, 5, j * P:(j + 1) * P], e12[:, 1, 0, j * P:(j + 1) * P])
                last.then_inc(sem("aT_acc"), 1)
                pump(1)
                pe.wait_ge(sem("aT_copied"), at("aT_copied", l, 2 * h + 2))
                v = slice(h * P, (h + 1) * P)
                pe.matmul(ps[:, 4, 0:P], aT[:, 3, :], vv[:, 0, v], start=True, stop=True)
                for t in (1, 2):
                    for j in range(3):
                        vals = vc[:, h, :] if j == 0 else vv[:, j, v]
                        last = pe.matmul(ps[:, 4, t * P:(t + 1) * P], aT[:, (0 if t == 1 else 4) + j, :], vals,
                                         start=j == 0, stop=j == 2)
                last.then_inc(sem("o_acc"), 1)

            pump(4)
            for h in range(HEADS):
                if h < 2:
                    pe.wait_ge(sem("exp_done"), at("exp_done", l, 3 * HEADS))
                    out = ps[:, 6 + (R_YB + h) % 2, :]
                else:
                    out = aux_start(R_YB + h)
                if h == 0:
                    pe.wait_ge(sem("o_normed"), at("o_normed", l, 1))
                for t in range(NT):
                    last = transpose(out[:, t * P:(t + 1) * P], qk[:, h, 0, t, :])
                last.then_inc(sem("aux_ready"), 1)
            pump(4)
            pump(2)
            for k in range(KD):
                if k == KD // 2:
                    pump(6)
                out = aux_start(R_MERGED + k)
                pe.wait_ge(sem("merged_done"), at("merged_done", l, 5 if k < 4 else 6))
                for t in range(NT):
                    last = transpose(out[:, t * P:(t + 1) * P], merged[:, t, k * P:(k + 1) * P])
                last.then_inc(sem("aux_ready"), 1)
            pump(PAIRS_OUT)

            norm_transposes(1, R_NORM2)
            out = None
            r = R_BACK
            for t in range(NT):
                for half in range(2):
                    for s, src in enumerate((hTh, hTl)):
                        out = aux_start(r)
                        if r == R_BACK:
                            pe.wait_ge(sem("hT_ready"), at("hT_ready", l, 2 * KD))
                        for k in range(4):
                            last = transpose(out[:, k * P:(k + 1) * P],
                                             src[:, 4 * half + k, t * P:(t + 1) * P].bitcast(F32))
                        last.then_inc(sem("aux_ready"), 1)
                        r += 1
            out = aux_start(R_LOGITS)
            for t in range(NT):
                c = slice(t * P, (t + 1) * P)
                for k in range(KD):
                    last = mm3(out[:, t * NE:(t + 1) * NE], (hTh[:, k, c], hTl[:, k, c]),
                               (rwh[:, k, :], rwl[:, k, :]), start=k == 0, stop=k == KD - 1)
            last.then_inc(sem("aux_ready"), 1)
            out = aux_start(R_SLOTS)
            pe.wait_ge(sem("mask_done"), at("mask_done", l, 1))
            for t in range(NT):
                for s in range(t + 1):
                    pe.matmul(out[:, t * NE:(t + 1) * NE], tri[:, 0 if s == t else 1, :], mask[:, s, :],
                              start=s == 0, stop=s == t)
            for s in range(NT):
                last = pe.matmul(out[:, NT * NE:(NT + 1) * NE], tri[:, 1, :], mask[:, s, :],
                                 start=s == 0, stop=s == NT - 1)
            last.then_inc(sem("aux_ready"), 1)

            def gather(e, half):
                if half == 0:
                    pe.wait_ge(sem("pick_ready"), at("pick_ready", l, 1) + e)
                for k in range(4 * half, 4 * half + 4):
                    o = ps[:, half, (k % 4) * P:(k % 4 + 1) * P]
                    for s in range(2):
                        for t in range(NT):
                            last = pe.matmul(o, h2[:, s, t, k * P:(k + 1) * P], pick[:, t, :],
                                             start=s == 0 and t == 0, stop=s == 1 and t == NT - 1)
                if half:
                    last.then_inc(sem("X_acc"), 1)

            def turn_pick():
                for t in range(NT):
                    last = transpose(ps[:, 6, t * P:(t + 1) * P], pick[:, t, :].bitcast(F32))
                last.then_inc(sem("PT_acc"), 1)

            def combine(e, odd, c):
                t, half = c // 2, c % 2
                if c >= 2:
                    pe.wait_ge(sem("comb_done"), at("comb_done", l, c - 1) + e * 6)
                for s in range(2):
                    last = pe.matmul(ps[:, 6 + c % 2, :], pickT[:, odd, t, :],
                                     oe[:, s, half * W:(half + 1) * W], start=s == 0, stop=s == 1)
                last.then_inc(sem("comb_acc"), 1)

            def expert(e, odd, first=False, last_one=False):
                pe.wait_ge(sem("xe_ready"), at("xe_ready", l, 1) + e)
                for q in range(8):
                    name, value = lo_at(l, e, q)
                    pe.wait_ge(sem(name), value)
                    for i in range(2):
                        k = 2 * (q % 4) + i
                        last = mm3(ps[:, 2 + q // 4, :], (xeT[:, 0, k, :], xeT[:, 1, k, :]),
                                   (wxh[:, q % RING_MOE, i, :], wxl[:, q % RING_MOE, i, :]), start=k == 0, stop=k == KD - 1)
                    last.then_inc(sem("pair_used"), 1)
                    if q >= 2 and not first:
                        if q == 2:
                            pe.wait_ge(sem("out_ready"), at("out_ready", l, 0) + e)
                            pe.wait_ge(sem("PT_done"), at("PT_done", l, 1) + e)
                        combine(e - 1, 1 - odd, q - 2)
                if not last_one:
                    gather(e + 1, 0)
                pe.wait_ge(sem("a_done"), at("a_done", l, 1) + e)
                if not first:
                    pe.wait_ge(sem("comb_done"), at("comb_done", l, 0) + e * 6)
                for k in range(4):
                    last = transpose(ps[:, 7, k * P:(k + 1) * P], ae[:, k * P:(k + 1) * P])
                last.then_inc(sem("eT_acc"), 1)
                if not last_one:
                    gather(e + 1, 1)
                    if first:
                        pe.wait_ge(sem("PT_done"), at("PT_done", l, 1))
                    turn_pick()
                pe.wait_ge(sem("eT_ready"), at("eT_ready", l, 1) + e)
                for q in range(8, PAIRS_EXPERT):
                    name, value = lo_at(l, e, q)
                    pe.wait_ge(sem(name), value)
                    for i in range(2):
                        k = 2 * (q % 2) + i
                        last = mm3(ps[:, 4 + (q - 8) // 2, :], (eaT[:, 0, k, :], eaT[:, 1, k, :]),
                                   (wxh[:, q % RING_MOE, i, :], wxl[:, q % RING_MOE, i, :]), start=k == 0, stop=k == 3)
                    last.then_inc(sem("pair_used"), 1)

            pe.wait_ge(sem("h2_ready"), at("h2_ready", l, 1))
            pe.wait_ge(sem("evac_dve"), at("evac_dve", l, 8))
            pe.wait_ge(sem("slot_done"), at("slot_done", l, 1))
            gather(0, 0)
            gather(0, 1)
            turn_pick()
            expert_loop(pe, expert)
            pe.wait_ge(sem("out_ready"), at("out_ready", l, NE))
            for c in range(6):
                combine(NE - 1, (NE - 1) % 2, c)

            def turn(e, b):
                over_dve = sem(f"over_dve{l}")
                over_pe = sem(f"over_pe{l}")

                def wait_dve(k):
                    pe.wait_ge(over_dve, over_at("dve", e, b, k))

                def chunk(i):
                    wait_dve(OVER_DVE[f"c{i}"])
                    for k in range(4):
                        s = (xeT if i < 4 else eaT)
                        j = k + (4 * (i % 2) if i < 4 else 0)
                        last = mm3(ps[:, (2, 2, 3, 3, 4, 5)[i], :], (s[:, 0, j, :], s[:, 1, j, :]),
                                   (wh[:, k // 2, k % 2, :], wl[:, k // 2, k % 2, :]),
                                   start=k == 0 and i in (0, 2, 4, 5), stop=k == 3 and i in (1, 3, 4, 5))
                    last.then_inc(over_pe, 1)

                wait_dve(OVER_DVE["pick"])
                for k in range(KD):
                    o = ps[:, k // 4, (k % 4) * P:(k % 4 + 1) * P]
                    for s in range(2):
                        for t in range(NT):
                            pe.matmul(o, h2[:, s, t, k * P:(k + 1) * P], pick[:, t, :],
                                      start=s == 0 and t == 0, stop=s == 1 and t == NT - 1)
                for t in range(NT):
                    last = transpose(ps[:, 6, t * P:(t + 1) * P], pick[:, t, :].bitcast(F32))
                last.then_inc(over_pe, 1)
                for i in range(4):
                    chunk(i)
                wait_dve(OVER_DVE["a"])
                for k in range(4):
                    last = transpose(ps[:, 7, k * P:(k + 1) * P], ae[:, k * P:(k + 1) * P])
                last.then_inc(over_pe, 1)
                chunk(4)
                chunk(5)
                for c in range(6):
                    wait_dve(OVER_DVE["out_lo"] if c < 2 else OVER_DVE["part"] + c - 2)
                    for s in range(2):
                        last = pe.matmul(ps[:, 6 + c % 2, :], pickT[:, 0, c // 2, :],
                                         oe[:, s, (c % 2) * W:(c % 2 + 1) * W], start=s == 0, stop=s == 1)
                    last.then_inc(over_pe, 1)

            second_pass(pe, l, turn)

    def scalar_program(act):
        chain = Chain(act, "act_chain")
        link = chain.link

        def hi(l, p):
            c = p // 2
            act.wait_ge(landed[c % RAW], chunk_at(l, c))
            act.wait_ge(sem("pair_used"), at("pair_used", l, p - RING + 1))
            s = 2 * (p % 2)
            act.activation(wh[:, p % RING, :, :], raw[:, c % RAW, s:s + 2, :], ACT.Copy
                           ).then_inc(sem("hi_done"), 1)

        def root(name, l, k, out, in_):
            act.wait_ge(sem(name[0]), at(name[0], l, k))
            act.activation(out, in_, ACT.Sqrt).then_inc(sem(name[1]), 1)

        for dst, src in const_loads():
            act.dma_start(dst, src).then_inc(sem("const_in"), 16)
        act.wait_ge(sem("const_in"), 16 * N_CONST)
        act.wait_ge(sem("crow_acc"), 1)
        act.activation(csil[:, :], ps[:, 0, 0:16], ACT.Silu).then_inc(sem("csil_done"), 1)
        act.wait_ge(sem("csil_done"), 1)
        for g in range(2):
            act.activation(cs[:, :, g], csil[:, 8 - 8 * g:16 - 8 * g], ACT.Copy).then_inc(sem("cs_hi"), 1)
        act.activation(rwh[:, :, :], rw[:, :, :], ACT.Copy).then_inc(sem("cs_hi"), 1)

        for l in range(DEPTH):
            act.wait_ge(sem("x_ready"), at("x_ready", l, 0))
            rows = [(srow[0:8, :], io["norm1_w"][bass.ds(l, 1), :].rearrange("a (k p) -> (a k) p", p=P)),
                    (srow[8:16, :], io["norm2_w"][bass.ds(l, 1), :].rearrange("a (k p) -> (a k) p", p=P)),
                    (srow[16:24, :], io["a_b_s"][bass.ds(l, 1), :, :].rearrange("a g p -> (a g) p")),
                    (srow[24:25, :], io["subln_w"][bass.ds(l, 1), :]),
                    (anorm[:, :], io["a_norm_w"][bass.ds(l, 1), :].broadcast_to([P, W])),
                    (lamv[:, :, :], io["lambda_qk"][bass.ds(l, 1), :, :].broadcast_to([P, 4, DQ])),
                    (ws[:, :, :], io["a_w_s"][bass.ds(l, 1), :, :, :].rearrange("a g p q -> p (a g) q")),
                    (rope0[:, :, :, :], io["t_rope"]),
                    (modrow[4:5, :, :], io["b_mod"][bass.ds(l, 1), :].rearrange("a (n w) -> a n w", w=W))]
            for dst, src in rows:
                act.dma_start(dst, src).then_inc(sem("small_in"), 16)
            for i, name in enumerate(("q_norm_w", "k_norm_w")):
                for m in range(MAPS):
                    act.dma_start(qkn[:, i, m, :], io[name][bass.ds(l, 1), :].broadcast_to([P, DQ])
                                  ).then_inc(sem("qkn_in"), 16)
            for dst, src in ((dft_lat, io["t_dft_lat"]), (dft_pr, io["t_dft_pr"]), (dft_ch, io["t_dft_ch"])):
                act.dma_start(dst[tuple([slice(None)] * len(dst.shape))], src).then_inc(sem("dft_in"), 16)

            if l == 0:
                act.wait_ge(sem("x_in"), 16 * NT)

            def norm_stats(which, wait=None):
                for t in range(NT):
                    if t:
                        act.wait_ge(sem("act_junk"), junk_n[0])
                    ins = act.activation(junk[:, :], x[:, t, :], ACT.Square, accum_out=st[:, t:t + 1])
                    if t < NT - 1:
                        junk_n[0] += 1
                        ins.then_inc(sem("act_junk"), 1)
                    else:
                        ins.then_inc(sem("sumsq"), 1)
                act.wait_ge(sem("meansq"), at("meansq", l, which + 1))
                act.activation(st[:, 6:9], st[:, 3:6], ACT.Sqrt).then_inc(sem("root"), 1)

            norm_stats(0)
            act.wait_ge(sem("lam_dot"), at("lam_dot", l, 1))
            act.activation(lam[:, 2:4], lam[:, 0:2], ACT.Exp).then_inc(sem("lam_exp"), 1)

            for n in range(MOD_BLOCKS):
                for q in range(4):
                    hi(l, 4 * n + q)
                    if q == 1 and n:
                        act.wait_ge(sem("mod_acc"), at("mod_acc", l, n))
                        act.activation(modrow[0:4, n - 1, :], ps[0:4, (n - 1) % 2, :], ACT.Copy
                                       ).then_inc(sem("modrow_done"), 1)
            n = MOD_BLOCKS
            act.wait_ge(sem("mod_acc"), at("mod_acc", l, n))
            act.activation(modrow[0:4, n - 1, :], ps[0:4, (n - 1) % 2, :], ACT.Copy).then_inc(sem("modrow_done"), 1)
            hi(l, PAIRS_MOD)
            hi(l, PAIRS_MOD + 1)
            hi(l, PAIRS_MOD + 2)
            for i in range(8):
                act.wait_ge(sem("gate_acc"), at("gate_acc", l, i + 1))
                act.activation(gbc[:, i // 4, i % 2, (i // 2 % 2) * W:(i // 2 % 2 + 1) * W], ps[:, 3 + i % 2, :],
                               ACT.Copy).then_inc(sem("gate_done"), 1)

            def split_hi(out, r, name, k, scale=None):
                act.wait_ge(sem("aux_ready"), at("aux_ready", l, r + 1))
                kw = {} if scale is None else dict(scale=scale)
                act.activation(out, ps[:, 6 + r % 2, 0:T], ACT.Copy if scale is None else ACT.Identity, **kw
                               ).then_inc(sem(name), 1)

            def norm_hi(which):
                for k in range(KD):
                    n = which * KD + k + 1
                    act.wait_ge(sem("full_done"), at("full_done", l, n))
                    act.activation(hTh[:, k, :], full[:, k % 2, :], ACT.Copy).then_inc(sem("hT_hi"), 1)

            norm_hi(0)

            done = [PAIRS_MOD + 3]

            def pump(n):
                for _ in range(n):
                    hi(l, done[0])
                    done[0] += 1

            def evac(u):
                kind, which, half, _ = USES[u]
                act.wait_ge(sem("acc_ready"), at("acc_ready", l, u + 1))
                beside = FIRST_BR <= u < FIRST_BR + 8
                base = 0 if beside else 3 * (u % 2)
                src = ps[:, base:base + NT, :]
                if kind == "gate":
                    n = (u - FIRST_BR) // 2
                    if n:
                        act.wait_ge(sem("merged_done"), at("merged_done", l, n))
                    act.activation(gs[:, :, :], src, ACT.Sigmoid).then_inc(sem("evac_act"), 1)
                elif which == 0:
                    act.activation(uv[:, :, 0:W], src, ACT.Gelu_apprx_tanh).then_inc(sem("evac_act"), 1)
                elif which == 1:
                    act.activation(uv[:, :, W:2 * W], src, ACT.Gelu_apprx_tanh).then_inc(sem("evac_act"), 1)
                elif which == 8:
                    act.activation(f_in[:, :, :], src, ACT.Copy).then_inc(sem("evac_act"), 1)
                elif which < 6:
                    s, h0 = (which - 2) // 2, 4 * (which % 2)
                    for t in range(NT):
                        ins = act.activation(qk[:, h0:h0 + 4, s, t, :],
                                             ps[:, base + t, :].rearrange("p (h d) -> p h d", h=4), ACT.Copy)
                    ins.then_inc(sem("evac_act"), 1)
                else:
                    c = (which - 6) * W
                    act.activation(vv[:, :, c:c + W], src, ACT.Copy).then_inc(sem("evac_act"), 1)

            pump(4 - 3)
            pump(2)
            evac(0)
            pump(4)
            evac(1)
            for t in range(NT):
                if t == 0:
                    act.wait_ge(sem("evac_act"), at("evac_act", l, 2))
                else:
                    act.wait_ge(sem("act_junk"), junk_n[0])
                ins = act.activation(junk[:, 0:W], uv[:, t, W:2 * W], ACT.Square, accum_out=st[:, t:t + 1])
                if t < NT - 1:
                    ins.then_inc(sem("act_junk"), 1)
                    junk_n[0] += 1
                else:
                    ins.then_inc(sem("v_sumsq"), 1)
            pump(1)
            act.wait_ge(sem("v_meansq"), at("v_meansq", l, 1))
            act.activation(st[:, 6:9], st[:, 3:6], ACT.Sqrt).then_inc(sem("v_root"), 1)
            pump(3)
            evac(2)
            pump(4)
            evac(3)
            pump(2)
            for i in range(4):
                split_hi(yaT[:, 0, i, :], R_YA + i, "ya_hi", i)
            pump(2)
            evac(4)
            for g in range(4):
                pump(1)
                split_hi(ycT[:, 0, g, :], R_DFT + 3 * g + 2, "yc_hi", g)
            act.wait_ge(sem("yc_hi"), at("yc_hi", l, 4))
            for dst, name in ((kc, "cache_k"), (vc, "cache_v")):
                act.dma_start(dst[:, :, :], io[name][0, bass.ds(l, 1), :, :, :].rearrange("a s h d -> s (a h) d")
                              ).then_inc(sem("cache_in"), 16)
            evac(5)
            pump(4)
            evac(6)
            i = 0
            for s in range(2):
                for t in range(NT):
                    if i:
                        act.wait_ge(sem("qk_summed"), (l * 6 + i))
                    else:
                        act.wait_ge(sem("evac_act"), at("evac_act", l, 7))
                        act.wait_ge(sem("dft_copied"), at("dft_copied", l, 4))
                    act.activation(qsq[:, :].rearrange("p (h d) -> p h d", h=HEADS), qk[:, :, s, t, :], ACT.Square
                                   ).then_inc(sem("qk_sumsq"), 1)
                    i += 1
                    if i == 3:
                        pump(2)
            act.wait_ge(sem("qk_meansq"), at("qk_meansq", l, 1))
            act.activation(qst[:, :, :], qst[:, :, :], ACT.Sqrt).then_inc(sem("qk_root"), 1)
            pump(2)
            evac(7)
            pump(5)
            u8 = N_IN - 1
            evac(u8)
            act.wait_ge(sem("evac_act"), at("evac_act", l, N_IN))
            act.dma_start(io["new_v"][0, bass.ds(l, 1), :, :, :].rearrange("a s h d -> s (a h) d"),
                          vv[:, 0, :].rearrange("p (h d) -> p h d", h=HEADS)).then_inc(sem("kv_out"), 16)
            act.wait_ge(sem("qk_normed"), at("qk_normed", l, 1))
            act.dma_start(io["new_k"][0, bass.ds(l, 1), :, :, :].rearrange("a s h d -> s (a h) d"),
                          qk[:, :, 1, 0, :]).then_inc(sem("kv_out"), 16)

            att_done = [0]
            ends = {4: FIRST_BR, 10: FIRST_BR + 2, 16: FIRST_BR + 4, 22: FIRST_BR + 6}
            assert done[0] == PAIRS_MOD + PAIRS_W_IN + RING

            def beside(n):
                for _ in range(n):
                    hi(l, done[0])
                    done[0] += 1
                    att_done[0] += 1
                    if att_done[0] in ends:
                        evac(ends[att_done[0]])

            for h in range(HEADS):
                act.wait_ge(sem("qkT_acc"), at("qkT_acc", l, h + 1))
                act.activation(qT[:, :], ps[:, 6, 0:T], ACT.Copy).then_inc(sem("qT_done"), 1)
                beside(1)
                for i, t in enumerate((1, 0, 2)):
                    act.wait_ge(sem("score_max"), at("score_max", l, 3 * h + max(i, 1) + 1))
                    for m in range(MAPS):
                        if t == 0:
                            out, src = e0[:, m, :], ps[:, 4 + m, T:4 * P]
                        else:
                            out, src = e12[:, t - 1, m, :], ps[:, (4 if t == 1 else 6) + m, 0:T]
                        ins = act.activation(out, src, ACT.Exp, bias=nmx[:, t, m:m + 1], scale=DQ ** -0.5,
                                             accum_out=es[:, t, m:m + 1])
                    ins.then_inc(sem("exp_done"), 1)
                beside(1)
                for i in range(2):
                    act.wait_ge(sem("aT_acc"), at("aT_acc", l, 2 * h + i + 1))
                    n = 4 if i == 0 else 3
                    act.activation(aT[:, 4 * i:4 * i + n, :],
                                   ps[:, 3 + 2 * i, 0:n * P].rearrange("p (k n) -> p k n", k=n), ACT.Copy
                                   ).then_inc(sem("aT_copied"), 1)
                beside(1)
            act.wait_ge(sem("o_copied"), at("o_copied", l, HEADS))
            for t in range(NT):
                if t:
                    act.wait_ge(sem("qk_summed2"), l * NT + t)
                act.activation(o_sq[:, :].rearrange("p (h d) -> p h d", h=HEADS), qk[:, :, 0, t, :], ACT.Square
                               ).then_inc(sem("o_sq"), 1)
            act.wait_ge(sem("o_meansq"), at("o_meansq", l, 1))
            act.activation(qst[:, 0:3, 0:8], qst[:, 0:3, 0:8], ACT.Sqrt).then_inc(sem("o_root"), 1)
            beside(1)
            evac(FIRST_BR + 8)
            for h in range(HEADS):
                split_hi(ybT[:, h, 0, :], R_YB + h, "yb_hi", h, scale=subc[:, 0:1])
            for _ in range(4):
                hi(l, done[0])
                done[0] += 1
            for _ in range(4):
                hi(l, done[0])
                done[0] += 1
            for k in range(4):
                split_hi(mT[:, 0, k, :], R_MERGED + k, "mT_hi", k)
            evac(FIRST_BR + 10)
            end = PAIRS_MOD + PAIRS_W_IN + PAIRS_BR
            while done[0] < end + 2:
                hi(l, done[0])
                done[0] += 1
            for k in range(4, KD):
                split_hi(mT[:, 0, k, :], R_MERGED + k, "mT_hi", k)
            while done[0] < end + PAIRS_OUT:
                hi(l, done[0])
                done[0] += 1
            assert done[0] == PAIRS_MOD + PAIRS_DENSE

            act.wait_ge(sem("x_mid"), at("x_mid", l, 1))
            norm_stats(1)
            norm_hi(1)
            def expert_hi(e, q):
                j = q // 2
                act.wait_ge(landed[j % RAW], expert_chunk_at(l, e, j))
                if isinstance(e, int) and e == 0 and q < RING:
                    act.wait_ge(sem("pair_used"), used_at(l, e, q - RING))
                elif not (isinstance(e, int) and e == 0 and q < RING_MOE):
                    act.wait_ge(sem("pair_used"), used_at(l, e, q - RING_MOE))
                s = 2 * (q % 2)
                act.activation(wxh[:, q % RING_MOE, :, :], raw[:, j % RAW, s:s + 2, :], ACT.Copy
                               ).then_inc(sem("hi_done"), 1)

            for q in range(RING):
                expert_hi(0, q)
            for i in range(2 * NT):
                r = R_BACK + 2 * i
                act.wait_ge(sem("aux_ready"), at("aux_ready", l, r + 1))
                act.activation(h2[:, 0, i // 2, (i % 2) * W:(i % 2 + 1) * W], ps[:, 6 + r % 2, :], ACT.Copy
                               ).then_inc(sem("h2h_done"), 1)
            act.wait_ge(sem("aux_ready"), at("aux_ready", l, R_LOGITS + 1))
            act.activation(s_r[:, :, :].rearrange("p t e -> p (t e)"), ps[:, 6 + R_LOGITS % 2, 0:NT * NE], ACT.Sigmoid
                           ).then_inc(sem("score_done"), 1)

            def gathered(e, odd):
                act.wait_ge(sem("X_acc"), at("X_acc", l, 1) + e)
                act.activation(xeT[:, 0, :, :], ps[:, 0:2, :].rearrange("p b (k n) -> p (b k) n", k=4), ACT.Copy
                               ).then_inc(sem("xe_hi"), 1)
                act.wait_ge(sem("PT_acc"), at("PT_acc", l, 1) + e)
                act.activation(pickT[:, odd, :, :], ps[:, 6, 0:T].rearrange("p (t n) -> p t n", t=NT), ACT.Copy
                               ).then_inc(sem("PT_done"), 1)

            def expert(e, odd, first=False, last_one=False):
                for q in range(4, 9):
                    expert_hi(e, q)
                act.wait_ge(sem("pair_used"), used_at(l, e, 3))
                act.activation(sg[:, :], ps[:, 2, :], ACT.Silu).then_inc(sem("silu_done"), 1)
                for q in range(9, 12 if last_one else 13):
                    expert_hi(e, q)
                act.wait_ge(sem("eT_acc"), at("eT_acc", l, 1) + e)
                act.activation(eaT[:, 0, :, :], ps[:, 7, :].rearrange("p (k n) -> p k n", k=4), ACT.Copy
                               ).then_inc(sem("eT_hi"), 1)
                if not last_one:
                    gathered(e + 1, 1 - odd)
                    for q in range(13, 16):
                        expert_hi(e, q)
                act.wait_ge(sem("pair_used"), used_at(l, e, PAIRS_EXPERT - 1))
                act.activation(oe[:, 0, :].rearrange("p (b n) -> p b n", b=2), ps[:, 4:6, :], ACT.Copy
                               ).then_inc(sem("out_hi"), 1)

            expert_hi(0, 3)
            gathered(0, 0)
            expert_loop(act, expert)

            def turn(e, b):
                over_act = sem(f"over_act{l}")

                def wait_pe(k):
                    act.wait_ge(sem(f"over_pe{l}"), over_at("pe", e, b, k))

                def chunk(i):
                    act.wait_ge(sem(f"over_dma{l}"), over_at("dma", e, b, 16 * (i + 1)))
                    wait_pe(OVER_PE["gathered"] if i == 0 else OVER_PE[f"c{i - 1}"])
                    act.activation(wh[:, 0:2, :, :].rearrange("p r i n -> p (r i) n"), raw[:, 0, :, :], ACT.Copy
                                   ).then_inc(over_act, 1)

                wait_pe(OVER_PE["gathered"])
                act.activation(xeT[:, 0, :, :], ps[:, 0:2, :].rearrange("p b (k n) -> p (b k) n", k=4), ACT.Copy
                               ).then_inc(over_act, 1)
                for i in range(4):
                    chunk(i)
                wait_pe(OVER_PE["c1"])
                act.activation(sg[:, :], ps[:, 2, :], ACT.Silu).then_inc(over_act, 1)
                wait_pe(OVER_PE["turned"])
                act.activation(eaT[:, 0, :, :], ps[:, 7, :].rearrange("p (k n) -> p k n", k=4), ACT.Copy
                               ).then_inc(over_act, 1)
                chunk(4)
                chunk(5)
                wait_pe(OVER_PE["c5"])
                act.activation(oe[:, 0, :].rearrange("p (b n) -> p b n", b=2), ps[:, 4:6, :], ACT.Copy
                               ).then_inc(over_act, 1)

            second_pass(act, l, turn)
        act.wait_ge(sem("kv_out"), at("kv_out", DEPTH - 1, 32))

    def gpsimd_program(pool):
        for l in range(DEPTH):
            for p in range(PAIRS_MOD, PAIRS_MOD + PAIRS_DENSE):
                s = 2 * (p % 2)
                pool.wait_ge(sem("hi_done"), at("hi_done", l, p + 1))
                pool.tensor_tensor(wl[:, p % RING, :, :], raw[:, p // 2 % RAW, s:s + 2, :],
                                   wh[:, p % RING, :, :].bitcast(F32), ALU.subtract).then_inc(sem("lo_pool"), 1)
            pool.wait_ge(sem("h2_ready"), at("h2_ready", l, 1))
            pool.memset(y[:, :, :], 0.0).then_inc(sem("y_zero"), 1)

            def expert(e, odd, first=False, last_one=False):
                for q in POOL_Q:
                    pool.wait_ge(sem("hi_done"), at("hi_done", l, PAIRS_MOD + PAIRS_DENSE + q + 1) + e * PAIRS_EXPERT)
                    pool.tensor_tensor(wxl[:, q % RING_MOE, :, :], raw[:, q // 2 % RAW, 2 * (q % 2):2 * (q % 2) + 2, :],
                                       wxh[:, q % RING_MOE, :, :].bitcast(F32), ALU.subtract).then_inc(sem("lo_pool"), 1)

            expert_loop(pool, expert)

    def vector_program(dve):
        chain = Chain(dve, "dve_chain")
        link = chain.link
        dve.sem_inc(sem("x_ready"), 1)

        def lo(l, p):
            s = 2 * (p % 2)
            dve.wait_ge(sem("hi_done"), at("hi_done", l, p + 1))
            dve.tensor_tensor(wl[:, p % RING, :, :], raw[:, p // 2 % RAW, s:s + 2, :],
                              wh[:, p % RING, :, :].bitcast(F32), ALU.subtract).then_inc(sem("lo_dve"), 1)

        dve.wait_ge(sem("cs_hi"), 3)
        for g in range(2):
            ins = dve.tensor_tensor(cs[:, :, 2 + g], csil[:, 8 - 8 * g:16 - 8 * g], cs[:, :, g].bitcast(F32),
                                    ALU.subtract)
        ins.then_inc(sem("cs_ready"), 1)
        dve.tensor_tensor(rwl[:, :, :], rw[:, :, :], rwh[:, :, :].bitcast(F32), ALU.subtract
                          ).then_inc(sem("cs_ready"), 1)

        for l in range(DEPTH):
            def aux(r):
                return ps[:, 6 + r % 2, :]

            def mean_root(width, which, n1, n2, n3):
                dve.wait_ge(sem(n1), at(n1, l, which + 1))
                dve.tensor_scalar(st[:, 3:6], st[:, 0:3], 1.0 / width, EPS, ALU.mult, ALU.add
                                  ).then_inc(sem(n2), 1)
                dve.wait_ge(sem(n3), at(n3, l, which + 1))
                link(dve.reciprocal(st[:, 9:12], st[:, 6:9]))

            def norm_rows(which):
                mean_root(D, which, "sumsq", "meansq", "root")
                for t in range(NT):
                    ins = dve.tensor_scalar(xn[:, t, :], x[:, t, :], st[:, 9 + t:10 + t], None, ALU.mult)
                ins.then_inc(sem("xn_done"), 1)

            def norm_cols(which, r0):
                for k in range(KD + 1):
                    if k < KD:
                        r = r0 + k
                        dve.wait_ge(sem("aux_ready"), at("aux_ready", l, r + 1))
                        if k >= 2:
                            dve.wait_ge(sem("hT_ready"), at("hT_ready", l, which * KD + k - 1))
                        dve.tensor_scalar(full[:, k % 2, 0:P], aux(r)[:, 0:P], scl[:, which, k, 0:1],
                                          shf[:, which, k, 0:1], ALU.mult, ALU.add).then_inc(sem("aux_free0"), 1)
                        dve.tensor_scalar(full[:, k % 2, P:T], aux(r)[:, P:T], scl[:, which, k, 1:2],
                                          shf[:, which, k, 1:2], ALU.mult, ALU.add).then_inc(sem("full_done"), 1)
                        dve.wait_ge(sem("full_done"), at("full_done", l, which * KD + k + 1))
                        dve.sem_inc(sem("aux_free"), 1)
                    if k:
                        j = k - 1
                        dve.wait_ge(sem("hT_hi"), at("hT_hi", l, which * KD + j + 1))
                        dve.tensor_tensor(hTl[:, j, :], full[:, j % 2, :], hTh[:, j, :].bitcast(F32), ALU.subtract
                                          ).then_inc(sem("hT_ready"), 1)

            def split_lo(out, hi_part, r, name, n, ready):
                dve.wait_ge(sem(name), at(name, l, n + 1))
                dve.tensor_tensor(out, aux(r)[:, 0:T], hi_part.bitcast(F32), ALU.subtract
                                  ).then_inc(sem("aux_free"), 1)
                dve.wait_ge(sem("aux_free"), at("aux_free", l, r + 1))
                dve.sem_inc(sem(ready), 1)

            dve.wait_ge(sem("small_in"), at("small_in", l, 16 * 9))
            dve.wait_ge(sem("qkn_in"), 64 * (l + 1))
            link(dve.tensor_tensor(lamv[:, 0:4:2, :], lamv[:, 0:4:2, :], lamv[:, 1:4:2, :], ALU.mult))
            dve.tensor_reduce(lam[:, 0:2], lamv[:, 0:4:2, :], AX.X, ALU.add).then_inc(sem("lam_dot"), 1)
            for i in range(2):
                for t in range(2):
                    dve.tensor_tensor(rope[:, i, t, 0, :], rope0[:, t, 0, :],
                                      qkn[:, i, :, :].rearrange("p m d -> p (m d)"), ALU.mult)
                    for j in range(2):
                        ins = dve.tensor_tensor(
                            rope[:, i, t, 1, :].rearrange("p (a j c) -> p a j c", j=2, c=16)[:, :, j, :],
                            rope0[:, t, 1, :].rearrange("p (a j c) -> p a j c", j=2, c=16)[:, :, j, :],
                            qkn[:, i, :, :].rearrange("p m d -> p (m d)").rearrange(
                                "p (a j c) -> p a j c", j=2, c=16)[:, :, 1 - j, :], ALU.mult)
            ins.then_inc(sem("rope_ready"), 1)
            norm_rows(0)
            for p in range(PAIRS_MOD):
                lo(l, p)
            dve.wait_ge(sem("lam_exp"), at("lam_exp", l, 1))
            link(dve.tensor_tensor(lam[:, 4:5], lam[:, 3:4], lam[:, 2:3], ALU.subtract))
            dve.tensor_tensor(lam[:, 5:6], lam[:, 4:5], laminit[:, l, 0:1], ALU.subtract
                              ).then_inc(sem("lam_ready"), 1)
            dve.wait_ge(sem("mcol_acc"), at("mcol_acc", l, 1))
            link(dve.tensor_copy(scol[:, :], ps[:, 2, 64:89]))
            mc = ps[:, 2, 0:64].rearrange("p (w k g) -> p w k g", w=4, g=2)
            for i in range(2):
                dve.tensor_copy(shf[:, i, :, :], mc[:, 2 * i, :, :])
                dve.scalar_tensor_tensor(scl[:, i, :, :], mc[:, 2 * i + 1, :, :], 1.0,
                                         scol[:, 8 * i:8 * i + 8].unsqueeze(2).to_broadcast([P, KD, 2]),
                                         ALU.add, ALU.mult)
            dve.tensor_scalar(subc[:, :], scol[:, 24:25], laminit[:, l, 1:2], None, ALU.mult
                              ).then_inc(sem("col_ready"), 1)
            dve.wait_ge(sem("col_ready"), at("col_ready", l, 1))
            norm_cols(0, R_NORM1)

            mean_root(W, 0, "v_sumsq", "v_meansq", "v_root")
            for t in range(NT):
                ins = dve.scalar_tensor_tensor(uv[:, t, W:2 * W], uv[:, t, W:2 * W], st[:, 9 + t:10 + t],
                                               anorm[:, :], ALU.mult, ALU.mult)
            ins.then_inc(sem("vn_done"), 1)
            for i in range(2):
                r = R_WS + i
                dve.wait_ge(sem("aux_ready"), at("aux_ready", l, r + 1))
                dve.tensor_copy(wsT[:, 4 * i:4 * i + 4, :], aux(r).rearrange("p (g n) -> p g n", g=4)
                                ).then_inc(sem("aux_free"), 1)
            for i in range(4):
                r = R_SV + i
                dve.wait_ge(sem("aux_ready"), at("aux_ready", l, r + 1))
                for j in range(2):
                    g = 2 * i + j
                    u = uv[:, :, g * 64:(g + 1) * 64]
                    ins = dve.scalar_tensor_tensor(u, aux(r)[:, j * 192:(j + 1) * 192].rearrange("p (t c) -> p t c", t=NT),
                                                   scol[:, 16 + g:17 + g], u, ALU.add, ALU.mult)
                ins.then_inc(sem("aux_free"), 1)
            dve.wait_ge(sem("aux_free"), at("aux_free", l, R_SV + 4))
            dve.sem_inc(sem("ya_tok"), 1)
            for i in range(4):
                split_lo(yaT[:, 1, i, :], yaT[:, 0, i, :], R_YA + i, "ya_hi", i, "ya_ready")
            for g in range(4):
                r = R_DFT + 3 * g
                dve.wait_ge(sem("aux_ready"), at("aux_ready", l, r + 1))
                if g:
                    dve.wait_ge(sem("aux_ready"), at("aux_ready", l, r))
                dve.tensor_copy(spec[:, :, P:T], aux(r).rearrange("p (s n) -> p s n", s=2)
                                ).then_inc(sem("aux_free"), 1)
                dve.wait_ge(sem("aux_ready"), at("aux_ready", l, r + 2))
                dve.tensor_copy(spec[:, :, 0:P], aux(r + 1)[:, 0:256].rearrange("p (s n) -> p s n", s=2)
                                ).then_inc(sem("aux_free"), 1)
                dve.wait_ge(sem("aux_free"), at("aux_free", l, r + 2))
                dve.sem_inc(sem("dft_copied"), 1)
                split_lo(ycT[:, 1, g, :], ycT[:, 0, g, :], r + 2, "yc_hi", g, "yc_ready")

            i = 0
            for s in range(2):
                for t in range(NT):
                    dve.wait_ge(sem("qk_sumsq"), at("qk_sumsq", l, i + 1))
                    dve.tensor_reduce(qst[:, i, :], qsq[:, :].rearrange("p (n d) -> p n d", d=DQ), AX.X, ALU.add
                                      ).then_inc(sem("qk_summed"), 1)
                    i += 1
            dve.wait_ge(sem("qk_summed"), 6 * (l + 1))
            dve.tensor_scalar(qst[:, :, :], qst[:, :, :], 1.0 / DQ, EPS, ALU.mult, ALU.add
                              ).then_inc(sem("qk_meansq"), 1)
            dve.wait_ge(sem("qk_root"), at("qk_root", l, 1))
            link(dve.reciprocal(qst[:, :, :], qst[:, :, :]))
            dve.wait_ge(sem("rope_ready"), at("rope_ready", l, 1))
            dve.wait_ge(sem("evac_act"), at("evac_act", l, 7))
            i = 0
            tmp = ropetmp
            for s in range(2):
                for t in range(NT):
                    v = qk[:, :, s, t, :]
                    r4 = qst[:, i, :].rearrange("p (h m) -> p h m", m=MAPS).unsqueeze(3).to_broadcast([P, HEADS, MAPS, DQ])
                    v4 = v.rearrange("p h (m d) -> p h m d", m=MAPS)
                    link(dve.tensor_tensor(v4, v4, r4, ALU.mult))
                    if t == 0:
                        w = qkn[:, s, :, :].rearrange("p m d -> p (m d)").unsqueeze(1).to_broadcast([P, HEADS, P])
                        ins = dve.tensor_tensor(v, v, w, ALU.mult)
                    else:
                        for j in range(2):
                            src = v.rearrange("p h (a j c) -> p h a j c", j=2, c=16)[:, :, :, 1 - j, :]
                            dst = tmp[:, :, :].rearrange("p h (a j c) -> p h a j c", j=2, c=16)[:, :, :, j, :]
                            sn = rope[:, s, t - 1, 1, :].rearrange("p (a j c) -> p a j c", j=2, c=16)[:, :, j, :]
                            ins = dve.tensor_tensor(dst, src, sn.unsqueeze(1).to_broadcast([P, HEADS, 4, 16]), ALU.mult)
                        link(ins)
                        cos = rope[:, s, t - 1, 0, :].unsqueeze(1).to_broadcast([P, HEADS, P])
                        link(dve.tensor_tensor(v, v, cos, ALU.mult))
                        ins = dve.tensor_tensor(v, v, tmp[:, :, :], ALU.add)
                        if i < 5:
                            link(ins)
                    i += 1
            ins.then_inc(sem("qk_normed"), 1)

            merge_at = {(1, 2): 0, (3, 2): 1, (5, 2): 2, (7, 2): 3}

            def merge(n):
                u = FIRST_BR + 2 * n + 1
                base = 0 if u < FIRST_BR + 8 else 3 * (u % 2)
                half = n % 2
                m = merged[:, :, half * W:(half + 1) * W]
                dve.wait_ge(sem("acc_ready"), at("acc_ready", l, u + 1))
                if n < 2:
                    dve.tensor_tensor(m, ps[:, base:base + NT, :], gs[:, :, :], ALU.mult).then_inc(sem("evac_dve"), 1)
                    dve.wait_ge(sem("evac_dve"), at("evac_dve", l, n + 1))
                    dve.sem_inc(sem("merged_done"), 1)
                else:
                    dve.tensor_tensor(gs[:, :, :], ps[:, base:base + NT, :], gs[:, :, :], ALU.mult
                                      ).then_inc(sem("evac_dve"), 1)
                    dve.wait_ge(sem("evac_dve"), at("evac_dve", l, n + 1))
                    dve.tensor_tensor(m, m, gs[:, :, :], ALU.add).then_inc(sem("merged_done"), 1)

            dve.wait_ge(sem("lam_ready"), at("lam_ready", l, 1))
            for h in range(HEADS):
                dve.wait_ge(sem("qkT_acc"), at("qkT_acc", l, h + 1))
                dve.tensor_copy(kT[:, :], ps[:, 7, :]).then_inc(sem("kT_done"), 1)
                for i, t in enumerate((1, 0, 2)):
                    if t != 0:
                        dve.wait_ge(sem("score_acc"), at("score_acc", l, 2 * h + t))
                    if t == 0:
                        src = ps[:, 4:6, T:4 * P]
                    else:
                        b = 4 if t == 1 else 6
                        src = ps[:, b:b + 2, 0:T]
                    link(dve.tensor_reduce(mx[:, t, :], src, AX.X, ALU.max))
                    dve.tensor_scalar(nmx[:, t, :], mx[:, t, :], -DQ ** -0.5, None, ALU.mult
                                      ).then_inc(sem("score_max"), 1)
                for i, t in enumerate((1, 0, 2)):
                    dve.wait_ge(sem("exp_done"), at("exp_done", l, 3 * h + i + 1))
                    link(dve.reciprocal(er[:, t, :], es[:, t, :]))
                    link(dve.tensor_tensor(er[:, t, 1:2], er[:, t, 1:2], lam[:, 5:6], ALU.mult))
                    a = e0 if t == 0 else e12[:, t - 1, :, :]
                    link(dve.tensor_scalar(a[:, 0, :], a[:, 0, :], er[:, t, 0:1], None, ALU.mult))
                    dve.scalar_tensor_tensor(a[:, 0, :], a[:, 1, :], er[:, t, 1:2], a[:, 0, :], ALU.mult, ALU.add
                                             ).then_inc(sem("diff_done"), 1)
                if h % 2 == 1:
                    merge(h // 2)
                dve.wait_ge(sem("o_acc"), at("o_acc", l, h + 1))
                dve.tensor_copy(qk[:, h, 0, :, :], ps[:, 4, 0:T].rearrange("p (t d) -> p t d", t=NT)
                                ).then_inc(sem("o_copied"), 1)
            for t in range(NT):
                dve.wait_ge(sem("o_sq"), l * NT + t + 1)
                dve.tensor_reduce(qst[:, t, 0:8], o_sq[:, :].rearrange("p (h d) -> p h d", h=HEADS), AX.X, ALU.add
                                  ).then_inc(sem("qk_summed2"), 1)
            dve.wait_ge(sem("qk_summed2"), NT * (l + 1))
            dve.tensor_scalar(qst[:, 0:3, 0:8], qst[:, 0:3, 0:8], 1.0 / P, EPS, ALU.mult, ALU.add
                              ).then_inc(sem("o_meansq"), 1)
            dve.wait_ge(sem("o_root"), at("o_root", l, 1))
            link(dve.reciprocal(qst[:, 0:3, 0:8], qst[:, 0:3, 0:8]))
            dve.wait_ge(sem("kv_out"), at("kv_out", l, 32))
            for t in range(NT):
                v = qk[:, :, 0, t, :]
                ins = dve.tensor_tensor(v, v, qst[:, t, 0:8].unsqueeze(2).to_broadcast([P, HEADS, P]), ALU.mult)
            ins.then_inc(sem("o_normed"), 1)
            for h in range(HEADS):
                r = R_YB + h
                dve.wait_ge(sem("yb_hi"), at("yb_hi", l, h + 1))
                dve.scalar_tensor_tensor(ybT[:, h, 1, :], aux(r)[:, 0:T], subc[:, 0:1], ybT[:, h, 0, :].bitcast(F32),
                                         ALU.mult, ALU.subtract).then_inc(sem("aux_free"), 1)
                dve.wait_ge(sem("aux_free"), at("aux_free", l, r + 1))
                dve.sem_inc(sem("yb_ready"), 1)
            merge(4)
            for k in range(4):
                split_lo(mT[:, 1, k, :], mT[:, 0, k, :], R_MERGED + k, "mT_hi", k, "mT_ready")
            merge(5)
            for k in range(4, KD):
                split_lo(mT[:, 1, k, :], mT[:, 0, k, :], R_MERGED + k, "mT_hi", k, "mT_ready")
            for half in range(2):
                u = len(USES) - 2 + half
                base = 3 * (u % 2)
                c = slice(half * W, (half + 1) * W)
                dve.wait_ge(sem("acc_ready"), at("acc_ready", l, u + 1))
                for t in range(NT):
                    ins = dve.tensor_tensor(gs[:, t, :], ps[:, base + t, :], gbc[:, 0, min(t, 1), c], ALU.mult)
                ins.then_inc(sem("evac_dve"), 1)
                dve.wait_ge(sem("evac_dve"), at("evac_dve", l, 7 + half))
                ins = dve.tensor_tensor(x[:, :, c], x[:, :, c], gs[:, :, :], ALU.add)
                if half:
                    ins.then_inc(sem("x_mid"), 1)
                else:
                    link(ins)
            norm_rows(1)
            norm_cols(1, R_NORM2)
            for i in range(2 * NT):
                r = R_BACK + 2 * i
                dve.wait_ge(sem("h2h_done"), at("h2h_done", l, i + 1))
                dve.wait_ge(sem("aux_free"), at("aux_free", l, r))
                dve.sem_inc(sem("aux_free"), 1)
                dve.wait_ge(sem("aux_ready"), at("aux_ready", l, r + 2))
                ins = dve.tensor_copy(h2[:, 1, i // 2, (i % 2) * W:(i % 2 + 1) * W], aux(r + 1)
                                      ).then_inc(sem("aux_free"), 1)
            dve.wait_ge(sem("aux_free"), at("aux_free", l, R_LOGITS))
            dve.sem_inc(sem("h2_ready"), 1)
            dve.wait_ge(sem("score_done"), at("score_done", l, 1))
            dve.sem_inc(sem("aux_free"), 1)
            sb, selv, gt, eq = rt[:, 0, 0:48], rt[:, 1, 0:48], rt[:, 2, :], rt[:, 3, :]
            rank, pair, grank, wgt, den = rt[:, 4, 0:48], rt[:, 5, 0:12], rt[:, 5, 16:28], rt[:, 6, 0:48], rt[:, 7, 0:6]
            link(dve.tensor_tensor(sb.rearrange("p (t e) -> p t e", t=NT), s_r[:, :, :],
                                   rb[:, :].unsqueeze(1).to_broadcast([P, NT, NE]), ALU.add))

            def ranks(vals, out, n):
                v = vals.rearrange("p (g i) -> p g i", i=EG)
                vi = v.unsqueeze(3).to_broadcast([P, n, EG, EG])
                vj = v.unsqueeze(2).to_broadcast([P, n, EG, EG])
                gv = gt[:, 0:n * EG * EG].rearrange("p (g i j) -> p g i j", i=EG, j=EG)
                ev = eq[:, 0:n * EG * EG].rearrange("p (g i j) -> p g i j", i=EG, j=EG)
                dve.tensor_tensor(gv, vj, vi, ALU.is_gt)
                link(dve.tensor_tensor(ev, vj, vi, ALU.is_equal))
                link(dve.tensor_tensor(ev, ev, rank_tri[:, :, :].unsqueeze(1).to_broadcast([P, n, EG, EG]), ALU.mult))
                link(dve.tensor_tensor(gv, gv, ev, ALU.add))
                link(dve.tensor_reduce(out.rearrange("p (g i) -> p g i", i=EG), gv, AX.X, ALU.add))

            ranks(sb, rank, 12)
            link(dve.tensor_scalar(selv, rank, 2.0, None, ALU.is_lt))
            link(dve.tensor_tensor(wgt, selv, sb, ALU.mult))
            link(dve.tensor_reduce(pair, wgt.rearrange("p (g i) -> p g i", i=EG), AX.X, ALU.add))
            ranks(pair, grank, NT)
            link(dve.tensor_scalar(grank, grank, 1.0, None, ALU.is_lt))
            m48 = mask[:, :, :].rearrange("p t e -> p (t e)")
            dve.tensor_tensor(m48.rearrange("p (g i) -> p g i", i=EG), selv.rearrange("p (g i) -> p g i", i=EG),
                              grank.unsqueeze(2).to_broadcast([P, 12, EG]), ALU.mult).then_inc(sem("mask_done"), 1)
            dve.wait_ge(sem("mask_done"), at("mask_done", l, 1))
            link(dve.tensor_tensor(wgt, s_r[:, :, :].rearrange("p t e -> p (t e)"), m48, ALU.mult))
            link(dve.tensor_reduce(den[:, 0:3], wgt.rearrange("p (t e) -> p t e", t=NT), AX.X, ALU.add))
            link(dve.reciprocal(den[:, 3:6], den[:, 0:3]))
            link(dve.tensor_tensor(gate[:, :, :], wgt.rearrange("p (t e) -> p t e", t=NT),
                                   den[:, 3:6].unsqueeze(2).to_broadcast([P, NT, NE]), ALU.mult))
            dve.wait_ge(sem("aux_ready"), at("aux_ready", l, R_SLOTS + 1))
            link(dve.scalar_tensor_tensor(slot[:, :, :].rearrange("p t e -> p (t e)"), aux(R_SLOTS)[:, 0:48], SLOT_BASE + 1.0, m48,
                                          ALU.add, ALU.mult))
            link(dve.tensor_scalar(slot[:, :, :], slot[:, :, :], -1.0, None, ALU.add))
            link(dve.tensor_reduce(cnt[:, 0:1], aux(R_SLOTS)[:, 48:64], AX.X, ALU.max))
            dve.tensor_scalar(flag[:, 0:1], cnt[:, 0:1], float(P - SLOT_BASE), None, ALU.is_gt).then_inc(sem("flag_ready"), 1)
            dve.sem_inc(sem("aux_free"), 1)
            dve.sem_inc(sem("slot_done"), 1)

            def expert_lo(e, q):
                if q % PAIRS_EXPERT in POOL_Q:
                    return
                dve.wait_ge(sem("hi_done"), at("hi_done", l, PAIRS_MOD + PAIRS_DENSE + q + 1) + e * PAIRS_EXPERT)
                dve.tensor_tensor(wxl[:, q % RING_MOE, :, :], raw[:, q // 2 % RAW, 2 * (q % 2):2 * (q % 2) + 2, :],
                                  wxh[:, q % RING_MOE, :, :].bitcast(F32), ALU.subtract).then_inc(sem("lo_dve"), 1)

            def make_pick(e):
                for t in range(NT):
                    ins = dve.tensor_scalar(pick[:, t, :], iota[:, :], slot[:, t, bass.ds(e, 1)], None, ALU.is_equal)
                ins.then_inc(sem("pick_ready"), 1)

            def gathered(e):
                dve.wait_ge(sem("xe_hi"), at("xe_hi", l, 1) + e)
                dve.tensor_tensor(xeT[:, 1, :, :], ps[:, 0:2, :].rearrange("p b (k n) -> p (b k) n", k=4),
                                  xeT[:, 0, :, :].bitcast(F32), ALU.subtract).then_inc(sem("xe_ready"), 1)

            def out_lo(e):
                dve.wait_ge(sem("out_hi"), at("out_hi", l, 1) + e)
                dve.tensor_tensor(oe[:, 1, :].rearrange("p (b n) -> p b n", b=2), ps[:, 4:6, :],
                                  oe[:, 0, :].bitcast(F32).rearrange("p (b n) -> p b n", b=2), ALU.subtract
                                  ).then_inc(sem("out_ready"), 1)

            def combine(e, c):
                t, half = c // 2, c % 2
                dst = y[:, t, half * W:(half + 1) * W]
                dve.wait_ge(sem("comb_acc"), at("comb_acc", l, c + 1) + e * 6)
                dve.scalar_tensor_tensor(dst, ps[:, 6 + c % 2, :], gate[:, t, bass.ds(e, 1)], dst, ALU.mult, ALU.add
                                         ).then_inc(sem("comb_done"), 1)

            def expert(e, odd, first=False, last_one=False):
                if not last_one:
                    dve.wait_ge(sem("PT_acc"), at("PT_acc", l, 1) + e)
                    make_pick(e + 1)
                expert_lo(e, 3)
                expert_lo(e, 4)
                for c in range(6):
                    if c < 5:
                        expert_lo(e, 5 + c)
                    if not first:
                        combine(e - 1, c)
                dve.wait_ge(sem("silu_done"), at("silu_done", l, 1) + e)
                dve.wait_ge(sem("pair_used"), used_at(l, e, 7))
                dve.tensor_tensor(ae[:, :], ps[:, 3, :], sg[:, :], ALU.mult).then_inc(sem("a_done"), 1)
                expert_lo(e, 10)
                dve.wait_ge(sem("eT_hi"), at("eT_hi", l, 1) + e)
                dve.tensor_tensor(eaT[:, 1, :, :], ps[:, 7, :].rearrange("p (k n) -> p k n", k=4),
                                  eaT[:, 0, :, :].bitcast(F32), ALU.subtract).then_inc(sem("eT_ready"), 1)
                expert_lo(e, 11)
                if not last_one:
                    gathered(e + 1)
                    for q in range(12, 15):
                        expert_lo(e, q)
                out_lo(e)

            dve.wait_ge(sem("flag_ready"), at("flag_ready", l, 1))
            make_pick(0)
            for q in range(3):
                expert_lo(0, q)
            gathered(0)
            dve.wait_ge(sem("y_zero"), at("y_zero", l, 1))
            expert_loop(dve, expert)
            for c in range(6):
                combine(NE - 1, c)
            dve.wait_ge(sem("comb_done"), at("comb_done", l, 6 * NE))

            def turn(e, b):
                over_dve = sem(f"over_dve{l}")

                def wait_act(k):
                    dve.wait_ge(sem(f"over_act{l}"), over_at("act", e, b, k))

                def wait_pe(k):
                    dve.wait_ge(sem(f"over_pe{l}"), over_at("pe", e, b, k))

                def chunk(i):
                    wait_act(OVER_ACT[f"c{i}"])
                    dve.tensor_tensor(wl[:, 0:2, :, :].rearrange("p r i n -> p (r i) n"), raw[:, 0, :, :],
                                      wh[:, 0:2, :, :].rearrange("p r i n -> p (r i) n").bitcast(F32), ALU.subtract
                                      ).then_inc(over_dve, 1)

                dve.tensor_scalar(cnt[:, 2:5], slot[:, :, bass.ds(e, 1)].rearrange("p t a -> p (t a)"),
                                  float(-P * b), None, ALU.add).then_inc(sem(f"over_col{l}"), 1)
                dve.tensor_copy(cnt[:, 5:8], gate[:, :, bass.ds(e, 1)].rearrange("p t a -> p (t a)")
                                ).then_inc(sem(f"over_col{l}"), 1)
                dve.wait_ge(sem(f"over_col{l}"), e * 4 + 2 * b)
                for t in range(NT):
                    ins = dve.tensor_scalar(pick[:, t, :], iota[:, :], cnt[:, 2 + t:3 + t], None, ALU.is_equal)
                ins.then_inc(over_dve, 1)
                wait_act(OVER_ACT["x_hi"])
                dve.tensor_tensor(xeT[:, 1, :, :], ps[:, 0:2, :].rearrange("p b (k n) -> p (b k) n", k=4),
                                  xeT[:, 0, :, :].bitcast(F32), ALU.subtract).then_inc(over_dve, 1)
                dve.tensor_copy(pickT[:, 0, :, :], ps[:, 6, 0:T].rearrange("p (t n) -> p t n", t=NT)
                                ).then_inc(over_dve, 1)
                for i in range(4):
                    chunk(i)
                wait_act(OVER_ACT["silu"])
                wait_pe(OVER_PE["c3"])
                dve.tensor_tensor(ae[:, :], ps[:, 3, :], sg[:, :], ALU.mult).then_inc(over_dve, 1)
                wait_act(OVER_ACT["a_hi"])
                dve.tensor_tensor(eaT[:, 1, :, :], ps[:, 7, :].rearrange("p (k n) -> p k n", k=4),
                                  eaT[:, 0, :, :].bitcast(F32), ALU.subtract).then_inc(over_dve, 1)
                chunk(4)
                chunk(5)
                wait_act(OVER_ACT["out_hi"])
                dve.tensor_tensor(oe[:, 1, :].rearrange("p (b n) -> p b n", b=2), ps[:, 4:6, :],
                                  oe[:, 0, :].bitcast(F32).rearrange("p (b n) -> p b n", b=2), ALU.subtract
                                  ).then_inc(over_dve, 1)
                for c in range(6):
                    t, half = c // 2, c % 2
                    dst = y[:, t, half * W:(half + 1) * W]
                    wait_pe(OVER_PE["part"] + c)
                    dve.scalar_tensor_tensor(dst, ps[:, 6 + c % 2, :], cnt[:, 5 + t:6 + t], dst, ALU.mult, ALU.add
                                             ).then_inc(over_dve, 1)
                dve.wait_ge(over_dve, over_at("dve", e, b, OVER_STEPS["dve"]))

            second_pass(dve, l, turn)
            for t in range(NT):
                ins = dve.tensor_tensor(y[:, t, :], y[:, t, :], gbc[:, 1, min(t, 1), :], ALU.mult)
            link(ins)
            dve.tensor_tensor(x[:, :, :], x[:, :, :], y[:, :, :], ALU.add).then_inc(sem("x_ready"), 1)

    junk_n = [0]
    o_sq = place("o_sq", [P, D], F32, r_z)
    ropetmp = place("ropetmp", [P, HEADS, P], F32, r_z)
    A = slice(None)

    def const_loads():
        return [
            (ident[:, :], io["t_ident"]), (tri[:, :, :], io["t_tri"]), (iota[:, :], io["t_iota"]),
            (rank_tri[:, :, :], io["t_rank_tri"]), (sel2[:, :], io["t_sel2"]), (selb[:, :, :], io["t_selb"]),
            (laminit[:, :, :], io["t_laminit"]),
            (crow[0:8, :], io["c"].rearrange("a (k p) -> (a k) p", p=P)),
            (crow[8:16, :], io["c_ctx"].rearrange("(k p) -> k p", p=P)),
            (rw[:, :, :], io["router_w"].rearrange("(k p) e -> p k e", p=P)),
            (rb[:, :], io["router_b"].rearrange("(a e) -> a e", a=1).broadcast_to([P, NE])),
        ]

    N_CONST = len(const_loads())
    with nc.Block() as block:
        block.sync(sync_program)
        block.tensor(tensor_program)
        block.scalar(scalar_program)
        block.gpsimd(gpsimd_program)
        block.vector(vector_program)


_INS = ['x_prompt', 'x_sample', 'cache_k', 'cache_v', 'c', 'c_ctx', 'w_mod', 'b_mod', 'norm1_w', 'norm2_w', 'w_in',
        'a_norm_w', 'a_w_s', 'a_b_s', 'q_norm_w', 'k_norm_w', 'lambda_qk', 'subln_w', 'w_br_a', 'w_br_b', 'w_br_c',
        'w_out', 'router_w', 'router_b', 'w_e_gate', 'w_e_up', 'w_e_down']
_OUTS = [("y_prompt", (1, 128, 1024)), ("y_sample", (1, 256, 1024)), ("new_k", (1, DEPTH, 128, 8, 128)),
         ("new_v", (1, DEPTH, 128, 8, 128))]


def tables():
    import numpy as np

    f = np.float32
    i = np.arange(P)
    t = {"t_ident": np.eye(P, dtype=f)}
    t["t_tri"] = np.stack([(i[:, None] < i[None, :]), np.ones((P, P), bool)], 1).astype(f)
    t["t_iota"] = np.broadcast_to(np.arange(P, dtype=f), (P, P)).copy()
    j = np.arange(EG)
    t["t_rank_tri"] = np.broadcast_to((j[None, :] < j[:, None]).astype(f), (P, EG, EG)).copy()
    rows = np.array([[1, 0], [0, 1], [1, 0], [0, 1], [1, 1]], f)
    t["t_sel2"] = rows
    t["t_selb"] = np.repeat(rows[:, :, None], P, 2)
    n = np.arange(2 * P)
    freq = (np.float32(10000.0) ** (-np.arange(16, dtype=f) / f(16))).astype(f)
    ang = np.stack([(n // 64).astype(f)[:, None] * freq, (n % 64).astype(f)[:, None] * freq], 1)
    cos, sin = np.cos(ang), np.sin(ang)
    c = np.stack([cos, cos], 2).reshape(2 * P, 64)
    s = np.stack([-sin, sin], 2).reshape(2 * P, 64)
    cs = np.stack([np.tile(c, (1, 2)), np.tile(s, (1, 2))], 1).astype(f)
    t["t_rope"] = cs.reshape(2, P, 2, P).transpose(1, 0, 2, 3).copy()
    t["t_laminit"] = np.broadcast_to(np.array([[v, 1 - v] for v in LAM_INIT], f), (P, DEPTH, 2)).copy()

    def dft(length):
        a = 2 * np.pi * (np.outer(np.arange(length), np.arange(length)) % length) / length
        return np.cos(a) / np.sqrt(length), -np.sin(a) / np.sqrt(length)

    c, s = dft(256)
    t["t_dft_lat"] = np.stack([c, s], 1).reshape(2, P, 2, 256).transpose(1, 0, 2, 3).astype(f).copy()
    c, s = dft(P)
    t["t_dft_pr"] = np.stack([c, s], 1).astype(f)
    t["t_dft_ch"] = np.stack([c, -s], 1).astype(f)
    return t


def kernel(**inputs):
    import numpy as np
    import concourse.bacc as bacc
    from concourse.bass_utils import run_bass_kernel_spmd as run

    nc = bacc.Bacc("TRN2", target_bir_lowering=False, num_devices=1)
    arrays, io = {}, {}
    for name in _INS:
        arrays[name] = np.ascontiguousarray(inputs[name])
    arrays.update(tables())
    for name, a in arrays.items():
        io[name] = nc.dram_tensor(name, a.shape, F32, kind="ExternalInput").ap()
    for name, shape in _OUTS:
        io[name] = nc.dram_tensor(name, shape, F32, kind="ExternalOutput").ap()
    build(nc, io)
    r = run(nc, [arrays], core_ids=[0])
    return tuple(r.results[0][name] for name, _ in _OUTS)
```

```python
import math

import concourse.bass as bass
from concourse import mybir

F32 = mybir.dt.float32
F32R = mybir.dt.float32r
I32 = mybir.dt.int32
ACT = mybir.ActivationFunctionType
ALU = mybir.AluOpType
AX = mybir.AxisListType

P = 128
DEPTH = 2
D = 1024
NT = 3
T = NT * P
KD = D // P
W = 512
IN_COLS = 7680
HEADS = 8
MAPS = 2
DQ = 64
EPS = 1e-6
NE = 16
EG = 4
RAW = 3
RING = 3
RING_MOE = 6
LAM_INIT = [0.8 - 0.6 * math.exp(-0.3 * l) for l in range(DEPTH)]

MOD_BLOCKS = 12
MOD_EARLY = 10
PAIRS_BLOCK = 4
MOD_FIRST, MOD_SLOTS, MOD_GATHER, MOD_BETWEEN = 2, 20, 32, 4
MOD_STATS = 16
W_IN_ORDER = [0, 1, 8, 2, 3, 4, 5, 6, 7]
BRANCHES = [("a", 0, 4), ("c", 2, 4), ("b", 1, 8)]
PAIRS_W_IN = 4 * len(W_IN_ORDER)
PAIRS_BR = sum(2 * (4 + s // 2) for _, _, s in BRANCHES)
PAIRS_OUT = 8
PAIRS_DENSE = PAIRS_W_IN + PAIRS_BR + PAIRS_OUT
PAIRS_EXPERT = 12
POOL_Q = (2, 3, 8, 9)


def early_blocks(l):
    return [(l, n) for n in range(MOD_EARLY)]


def beside_router(l):
    return [(l, n) for n in range(MOD_EARLY, MOD_BLOCKS)] + (early_blocks(l + 1) if l + 1 < DEPTH else [])


def lay_stream():
    dense, mod, moe, makers = [], [], [], []

    def add_mod(blocks):
        for i in range(PAIRS_BLOCK * len(blocks)):
            makers.append("lo_pool" if i % 2 else "lo_dve")

    add_mod(early_blocks(0))
    for l in range(DEPTH):
        dense.append(len(makers))
        makers.extend(["lo_pool"] * PAIRS_DENSE)
        mod.append(len(makers))
        add_mod(beside_router(l))
        moe.append(len(makers))
        makers.extend(["lo_pool" if q in POOL_Q else "lo_dve" for q in range(PAIRS_EXPERT)] * NE)
    counts, low = {}, []
    for name in makers:
        counts[name] = counts.get(name, 0) + 1
        low.append((name, counts[name]))
    return dense, mod, moe, low


DENSE0, MOD0, MOE0, LOW = lay_stream()
assert PAIRS_EXPERT % RING_MOE == 0 and (PAIRS_EXPERT // 2) % RAW == 0

USES = [("in", b, 0, 4) for b in W_IN_ORDER]
for _name, _g, _s in BRANCHES:
    for _h in range(2):
        USES.append(("gate", _g, _h, 4))
        USES.append(("br", _name, _h, _s // 2))
USES += [("out", 0, h, 4) for h in range(2)]
N_IN = len(W_IN_ORDER)
FIRST_BR = N_IN
ATT_PAIRS = 24

R_NORM1 = 0
R_WS = R_NORM1 + KD
R_SV = R_WS + 2
R_YA = R_SV + 4
R_DFT = R_YA + 4
AUX = R_DFT + 12
R_YB = AUX
R_MERGED = R_YB + HEADS
R_NORM2 = R_MERGED + KD
R_LOGITS = R_NORM2 + KD
R_BACK = R_LOGITS + 1
R_SLOTS = R_BACK + 4 * NT
AUX_ROUNDS = R_SLOTS + 1

PER = dict(
    mcol_acc=1, col_ready=1,
    sumsq=2, meansq=2, root=2, xn_done=2, full_done=2 * KD, hT_hi=2 * KD, hT_ready=2 * KD,
    aux_ready=AUX_ROUNDS, aux_free=AUX_ROUNDS,
    evac_act=N_IN + 6, evac_dve=8,
    v_sumsq=1, v_meansq=1, v_root=1, vn_done=1, ya_tok=1, ya_hi=4, ya_ready=4,
    yc_hi=4, yc_ready=4, dft_copied=4,
    qk_sumsq=6, qk_summed=6, qk_meansq=2, qk_root=2, qk_normed=1, rope_ready=1,
    lam_exp=1, lam_dot=1, lam_ready=1,
    qkT_acc=HEADS, qT_done=HEADS, kT_done=HEADS, score_acc=2 * HEADS, score_max=3 * HEADS,
    exp_done=3 * HEADS, diff_done=3 * HEADS, aT_acc=2 * HEADS, aT_copied=2 * HEADS,
    o_acc=HEADS, o_copied=HEADS, o_sq=NT, o_summed=NT, o_meansq=1, o_root=1, o_normed=1,
    yb_hi=HEADS, yb_ready=HEADS, merged_done=6, mT_hi=KD, mT_ready=KD, x_mid=NT,
    score_done=1, mask_done=1, slot_done=1, flag_ready=1,
    pick_ready=NE, X_acc=NE, PT_acc=NE, PT_done=NE, xe_hi=NE, xe_ready=NE, silu_done=NE,
    a_done=NE, eT_acc=NE, eT_hi=NE, eT_ready=NE, out_hi=NE, out_ready=NE,
    comb_acc=6 * NE, comb_done=6 * NE, y_zero=1, x_ready=NT,
    small_in=16 * 4, cache_in=16 * 2, kv_out=16 * 2, dft_in=16 * 3,
)
CREDIT = dict(x_ready=1)


OVER_PE = dict(gathered=1, c0=2, c1=3, c2=4, c3=5, turned=6, c4=7, c5=8, part=9)
OVER_ACT = dict(x_hi=1, c0=2, c1=3, c2=4, c3=5, silu=6, a_hi=7, c4=8, c5=9, out_hi=10)
OVER_DVE = dict(pick=1, x_lo=2, pickT=3, c0=4, c1=5, c2=6, c3=7, a=8, a_lo=9, c4=10, c5=11, out_lo=12, part=13)
OVER_STEPS = dict(pe=14, act=10, dve=18, dma=16 * 6)
SLOT_BASE = 0


def build(nc, io):
    sems = {}

    def sem(name):
        if name not in sems:
            sems[name] = nc.alloc_semaphore(name)
        return sems[name]

    def at(name, l, k):
        return l * PER[name] + CREDIT.get(name, 0) + k

    top = [(nc.sbuf_base + 63) // 64 * 64]

    def place(name, shape, dt, offset=None):
        size = 4 * math.prod(shape[1:])
        if offset is None:
            offset = top[0]
            top[0] += (size + 31) // 32 * 32
        return nc.alloc_sbuf_tensor_at(name, shape, dt, offset=offset)

    def room(size):
        offset = top[0]
        top[0] += size
        return offset

    x = place("x", [P, NT, D], F32)
    raw = place("raw", [P, RAW, 4, W], F32)
    wh_at = top[0]
    wh = place("wh", [P, RING, 2, W], F32R)
    hTh = place("hTh", [P, KD, T], F32R)
    wl_at = top[0]
    wl = place("wl", [P, RING, 2, W], F32R)
    hTl = place("hTl", [P, KD, T], F32R)
    assert 4 * KD * T == 4 * (RING_MOE - RING) * 2 * W
    wxh = place("wxh", [P, RING_MOE, 2, W], F32R, wh_at)
    wxl = place("wxl", [P, RING_MOE, 2, W], F32R, wl_at)
    gbc = place("gbc", [P, 2, 2, D], F32)
    r_uv, r_qk, r_f, r_vv = room(12288), room(24576), room(6144), room(12288)
    r_ya, r_yc, r_kc, r_z = room(12288), room(12288), room(8192), room(14336)
    uv = place("uv", [P, NT, 2 * W], F32, r_uv)
    merged = place("merged", [P, NT, D], F32, r_uv)
    xn = place("xn", [P, NT, D], F32, r_uv)
    qk = place("qk", [P, HEADS, 2, NT, P], F32, r_qk)
    ybT = place("ybT", [P, HEADS, 2, T], F32R, r_qk)
    modrow = place("modrow", [5, MOD_BLOCKS, W], F32, r_vv)
    vv = place("vv", [P, NT, D], F32, r_vv)
    f_in = place("f_in", [P, NT, W], F32, r_f)
    gs = place("gs", [P, NT, W], F32, r_f)
    yaT = place("yaT", [P, 2, 4, T], F32R, r_ya)
    ycT = place("ycT", [P, 2, 4, T], F32R, r_yc)
    mT = place("mT", [P, 2, KD, T], F32R, r_ya)
    junk = place("junk", [P, D], F32, r_yc)
    full = place("full", [P, 2, T], F32, r_yc + 4096)
    qsq = place("qsq", [P, D], F32, r_f)
    kc = place("kc", [P, HEADS, P], F32, r_kc)
    vc = place("vc", [P, HEADS, P], F32, r_kc + 4096)
    dft_lat = place("dft_lat", [P, 2, 2, 256], F32, r_kc)
    dft_pr = place("dft_pr", [P, 2, P], F32, r_kc + 4096)
    dft_ch = place("dft_ch", [P, 2, P], F32, r_kc + 5120)
    ws = place("ws", [P, 8, P], F32, r_z)
    wsT = place("wsT", [P, 8, P], F32, r_z + 4096)
    spec = place("spec", [P, 2, T], F32, r_z)
    anorm = place("anorm", [P, W], F32, r_z + 8192)
    rope = place("rope", [P, 2, 2, 2, P], F32, r_z + 10240)
    qT = place("qT", [P, T], F32, r_z)
    kT = place("kT", [P, 4 * P], F32, r_z + 1536)
    e0 = place("e0", [P, MAPS, P], F32, r_z + 3584)
    e12 = place("e12", [P, 2, MAPS, T], F32, r_z + 4608)
    aT = place("aT", [P, 7, P], F32, r_z + 10752)
    xeT = place("xeT", [P, 2, KD, 2 * P], F32R, r_ya + 8192)
    xeT1 = place("xeT1", [P, 2, KD, P], F32R, r_uv)
    eaT = place("eaT", [P, 2, 4, P], F32R, r_uv + 8192)
    h2 = place("h2", [P, 2, NT, D], F32R, r_qk)
    y = place("y", [P, NT, D], F32, r_vv)
    pick = place("pick", [P, NT, 2, 2 * P], F32R, r_f)
    pick1 = place("pick1", [P, NT, P], F32R, r_f)
    pickT = place("pickT", [P, 2, NT, P], F32R, r_kc + 4096)
    oe = place("oe", [P, 2, D], F32R, r_ya)
    sg = place("sg", [P, W], F32, r_kc)
    ae = place("ae", [P, W], F32, r_kc + 2048)
    rt = place("rt", [P, 8, 192], F32, r_z)

    ident = place("ident", [P, P], F32)
    tri = place("tri", [P, 2, P], F32)
    iota = place("iota", [P, P], F32)
    rank_tri = place("rank_tri", [P, EG, EG], F32)
    sel2 = place("sel2", [5, 2], F32)
    selb = place("selb", [5, 2, P], F32)
    rope0 = place("rope0", [P, 2, 2, P], F32, r_yc + 9216)
    crow = place("crow", [16, P], F32, r_yc + 7168)
    csil = place("csil", [P, 16], F32)
    cs = place("cs", [P, KD, 4], F32R)
    rw = place("rw", [P, KD, NE], F32, r_yc + 7680)
    rwh = place("rwh", [P, KD, NE], F32R)
    rwl = place("rwl", [P, KD, NE], F32R)
    rb = place("rb", [P, NE], F32)
    srow = place("srow", [25, P], F32, r_yc + 11264)
    scol = place("scol", [P, 25], F32)
    qkn = place("qkn", [P, 2, MAPS, DQ], F32)
    lamv = place("lamv", [P, 4, DQ], F32, r_yc + 8192)
    laminit = place("laminit", [P, DEPTH, 2], F32)
    lam = place("lam", [P, 8], F32)
    scl = place("scl", [P, 2, KD, 2], F32)
    shf = place("shf", [P, 2, KD, 2], F32)
    st = place("st", [P, 16], F32)
    qst = place("qst", [P, 6, 16], F32)
    mx = place("mx", [P, 3, MAPS], F32)
    nmx = place("nmx", [P, 3, MAPS], F32)
    es = place("es", [P, 3, MAPS], F32)
    er = place("er", [P, 3, MAPS], F32)
    subc = place("subc", [P, 1], F32)
    s_r = place("s_r", [P, NT, NE], F32)
    slot = place("slot", [P, NT, NE], F32)
    mask = place("mask", [P, NT, NE], F32)
    gate = place("gate", [P, NT, NE], F32)
    cnt = place("cnt", [P, 8], F32)
    flag = place("flag", [P, 2], I32)
    assert top[0] <= nc.sbuf_usable_end, (top[0], nc.sbuf_usable_end)

    ps = nc.alloc_psum_tensor("ps", [P, 8, W], F32)

    w_mod = io["w_mod"].rearrange("l k n -> (l k) n")
    w_in = io["w_in"].rearrange("l k n -> (l k) n")
    w_out = io["w_out"].rearrange("l k n -> (l k) n")
    w_br = {b: io["w_br_" + b].rearrange("l k n -> (l k) n") for b in "abc"}
    w_eg = io["w_e_gate"].rearrange("l e k n -> (l e k) n")
    w_eu = io["w_e_up"].rearrange("l e k n -> (l e k) n")
    w_ed = io["w_e_down"].rearrange("l e k n -> (l e k) n")

    class Chain:

        def __init__(self, eng, name):
            self.eng, self.sem, self.n = eng, nc.alloc_semaphore(name), 0

        def link(self, ins):
            self.n += 1
            ins.then_inc(self.sem, 1)
            self.eng.wait_ge(self.sem, self.n)

    def over_at(eng, e, b, k):
        return e * (2 * OVER_STEPS[eng]) + ((b - 1) * OVER_STEPS[eng] + k)

    def second_pass(eng, l, turn):
        eng.wait_ge(sem("flag_ready"), at("flag_ready", l, 1))
        over = eng.value_load(flag[0:1, 0:1], min_val=0, max_val=1)
        with eng.If(over > 0):
            with eng.Fori(0, NE) as e:
                for b in (1, 2):
                    turn(e, b)
            eng.wait_ge(sem(f"over_dve{l}"), 2 * NE * OVER_STEPS["dve"])
        eng.end_ifs()

    def expert_loop(eng, expert):
        expert(0, 0, 0, first=True)
        expert(1, 1, 0)
        with eng.Fori(0, (NE - 4) // 4) as i:
            expert(i * 4 + 2, 0, 1)
            expert(i * 4 + 3, 1, 1)
            expert(i * 4 + 4, 0, 0)
            expert(i * 4 + 5, 1, 0)
        expert(NE - 2, 0, 1, last_pair=True)
        expert(NE - 1, 1, 1, last_pair=True, last_one=True)

    landed = [sem(f"chunk_landed{i}") for i in range(RAW)]

    def landed_at(c):
        return 16 * (c // RAW + 1)

    def block_pair(l, n):
        if l == 0 and n < MOD_EARLY:
            first = PAIRS_BLOCK * n
        elif n < MOD_EARLY:
            first = MOD0[l - 1] + PAIRS_BLOCK * (MOD_BLOCKS - MOD_EARLY + n)
        else:
            first = MOD0[l] + PAIRS_BLOCK * (n - MOD_EARLY)
        return first, MOD_BLOCKS * l + n

    def use_end(l, u):
        return DENSE0[l] + sum(use[3] for use in USES[:u + 1])

    CHUNKS_EXPERT = PAIRS_EXPERT // 2

    def used_at(l, e, q):
        return e * PAIRS_EXPERT + (MOE0[l] + q + 1)

    def lo_at(l, e, q):
        if q < 0:
            q, e = q + PAIRS_EXPERT, e - 1
        name, value = LOW[MOE0[l] + q]
        per = sum(1 for i in range(PAIRS_EXPERT) if (i in POOL_Q) == (name == "lo_pool"))
        return name, e * per + value

    def expert_chunk(l, e, j):
        c = MOE0[l] // 2 + j
        return c % RAW, e * (16 * (CHUNKS_EXPERT // RAW)) + landed_at(c)

    def sync_program(sp):
        def split(l, e, j):
            name, value = lo_at(l, e, 2 * j + 1)
            sp.wait_ge(sem(name), value)

        def load(c, src, row, col):
            if c >= RAW:
                for name, value in dict(LOW[2 * (c - RAW) + i] for i in range(2)).items():
                    sp.wait_ge(sem(name), value)
            sp.dma_start(raw[:, c % RAW, :, :],
                         src[bass.ds(row, 4 * P), col:col + W].rearrange("(k p) n -> p k n", p=P)
                         ).then_inc(landed[c % RAW], 16)

        def load_blocks(c, blocks):
            for l, n in blocks:
                for k in range(2):
                    load(c, w_mod, l * D + k * W, n * W)
                    c += 1

        load_blocks(0, early_blocks(0)[:2])
        for t in range(NT):
            src = io["x_prompt"][0, :, :] if t == 0 else io["x_sample"][0, (t - 1) * P:t * P, :]
            sp.dma_start(x[:, t, :], src).then_inc(sem("x_in"), 16)
        load_blocks(4, early_blocks(0)[2:])
        for l in range(DEPTH):
            c = DENSE0[l] // 2
            for kind, which, half, pairs in USES:
                for k in range(pairs // 2):
                    if kind == "in":
                        load(c, w_in, l * D + k * W, which * W)
                    elif kind == "gate":
                        load(c, w_in, l * D + k * W, IN_COLS - 3 * D + which * D + half * W)
                    elif kind == "br":
                        load(c, w_br[which], l * pairs * 2 * P + k * W, half * W)
                    else:
                        load(c, w_out, l * D + k * W, half * W)
                    c += 1
            load_blocks(MOD0[l] // 2, beside_router(l))

            def expert(e, odd, pair, first=False, last_pair=False, last_one=False):
                for j in range(CHUNKS_EXPERT):
                    place = expert_chunk(l, 0, j)[0]
                    if first and j < RAW:
                        for name, value in dict(LOW[MOE0[l] + 2 * (j - RAW) + i] for i in range(2)).items():
                            sp.wait_ge(sem(name), value)
                    else:
                        split(l, e, j - RAW)
                    if j < 4:
                        src, row, col = (w_eg, w_eu)[j // 2], (l * NE + e) * D + j % 2 * W, 0
                    else:
                        src, row, col = w_ed, (l * NE + e) * W, (j - 4) * W
                    sp.dma_start(raw[:, place, :, :],
                                 src[bass.ds(row, 4 * P), col:col + W].rearrange("(k p) n -> p k n", p=P)
                                 ).then_inc(landed[place], 16)

            expert_loop(sp, expert)

            def turn(e, b):
                for i in range(6):
                    sp.wait_ge(sem(f"over_dve{l}"), over_at("dve", e, b, OVER_DVE["pick"] if i == 0 else OVER_DVE[f"c{i - 1}"]))
                    src = (w_eg, w_eg, w_eu, w_eu, w_ed, w_ed)[i]
                    row = (l * NE + e) * (D if i < 4 else W) + (i % 2 * W if i < 4 else 0)
                    col = 0 if i < 4 else (i % 2) * W
                    sp.dma_start(raw[:, 0, :, :], src[bass.ds(row, 4 * P), col:col + W].rearrange("(k p) n -> p k n", p=P)
                                 ).then_inc(sem(f"over_dma{l}"), 16)

            second_pass(sp, l, turn)
        for t in range(NT):
            sp.wait_ge(sem("x_ready"), at("x_ready", DEPTH - 1, t + 1))
            dst = io["y_prompt"][0, :, :] if t == 0 else io["y_sample"][0, (t - 1) * P:t * P, :]
            sp.dma_start(dst, x[:, t, :]).then_inc(sem("y_out"), 16)
        sp.wait_ge(sem("y_out"), 16 * NT)

    def tensor_program(pe):
        T3 = ((0, 0), (0, 1), (1, 0))

        def mm3(out, act_hl, w_hl, start, stop):
            for n, (i, j) in enumerate(T3):
                ins = pe.matmul(out, act_hl[i], w_hl[j], start=start and n == 0, stop=stop and n == 2)
            return ins

        def wait_pair(p):
            pe.wait_ge(sem(LOW[p][0]), LOW[p][1])

        def transpose(out, in_, **kw):
            n = in_.shape[0]
            return pe.transpose(out, in_, ident[0:n, 0:n])

        pe.wait_ge(sem("first_in"), 16 * 3)
        transpose(ps[:, 0, 0:16], crow[:, :]).then_inc(sem("crow_acc"), 1)
        pe.wait_ge(sem("cs_ready"), 1)

        gates = [0]
        COLUMNS = (0, 1, 2, 3, 6, 7, 8, 9)

        def spread(l, n, g):
            if n in COLUMNS and g == 0:
                for k in range(4):
                    o = 8 * COLUMNS.index(n) + 2 * k
                    last = pe.matmul(ps[:, 5, o:o + 2], modrow[:, n, k * P:(k + 1) * P], sel2[:, :],
                                     start=True, stop=True)
                if n == MOD_EARLY - 1:
                    last.then_inc(sem("mcol_acc"), 1)
            elif n not in COLUMNS:
                if gates[0]:
                    pe.wait_ge(sem("gate_done"), gates[0])
                gates[0] += 1
                pe.matmul(ps[:, 2, :], selb[:, g, :], modrow[:, n, :], start=True, stop=True
                          ).then_inc(sem("gate_acc"), 1)

        def modulation(blocks, cols_in):
            for i, (l, n) in enumerate(blocks):
                first, number = block_pair(l, n)
                if i >= 2:
                    pe.wait_ge(sem("modrow_done"), number - 1)
                for q in range(PAIRS_BLOCK):
                    p = first + q
                    wait_pair(p)
                    for j in range(2):
                        k = 2 * q + j
                        for w in (wh, wl):
                            last = pe.matmul(ps[0:4, 3 + n % 2, :], cs[:, k, :], w[:, p % RING, j, :],
                                             start=k == 0 and w is wh, stop=k == KD - 1 and w is wl)
                    last.then_inc(sem("pair_used"), 1)
                    if i and q >= 2:
                        if q == 2:
                            pe.wait_ge(sem("modrow_done"), number)
                        if i == 1 and q == 2:
                            pe.wait_ge(sem("cols_in"), cols_in)
                            pe.wait_ge(sem("const_in"), 16 * N_CONST)
                            if len(blocks) > MOD_BLOCKS - MOD_EARLY:
                                transpose(ps[:, 5, 64:89], srow[:, :])
                        spread(*blocks[i - 1], q - 2)
                    yield
            pe.wait_ge(sem("modrow_done"), number + 1)
            for g in range(2):
                spread(*blocks[-1], g)

        for _ in modulation(early_blocks(0), COLS_IN[0]):
            pass

        for l in range(DEPTH):
            def aux_start(r):
                if r >= 2:
                    pe.wait_ge(sem("aux_free"), at("aux_free", l, r - 1))
                return ps[:, 6 + r % 2, :]

            def norm_transposes(which, r0):
                for k in range(KD):
                    if which and k == 0:
                        pump_mod(MOD_FIRST)
                    out = aux_start(r0 + k)
                    if k == 0:
                        pe.wait_ge(sem("xn_done"), at("xn_done", l, which + 1))
                    for t in range(NT):
                        last = transpose(out[:, t * P:(t + 1) * P], xn[:, t, k * P:(k + 1) * P])
                    last.then_inc(sem("aux_ready"), 1)

            norm_transposes(0, R_NORM1)
            if l == 0:
                pe.wait_ge(sem("gate_done"), gates[0])
            pe.wait_ge(sem("col_ready"), at("col_ready", l, 1))

            def act_done(u):
                return sum(1 for k in USES[:u] if k[0] in ("in", "gate"))

            def dense():
                p = DENSE0[l]
                for u, (kind, which, half, pairs) in enumerate(USES):
                    beside = FIRST_BR <= u < FIRST_BR + 8
                    base = 0 if beside else 3 * (u % 2)
                    prev = u - 1 if beside else u - 2
                    if prev >= 0:
                        if USES[prev][0] in ("in", "gate"):
                            pe.wait_ge(sem("evac_act"), at("evac_act", l, act_done(prev + 1)))
                        else:
                            pe.wait_ge(sem("evac_dve"), at("evac_dve", l, prev + 1 - act_done(prev + 1)))
                    if u == FIRST_BR + 8:
                        pe.wait_ge(sem("o_copied"), at("o_copied", l, HEADS))
                    for q in range(pairs):
                        wait_pair(p)
                        for i in range(2):
                            k = 2 * q + i
                            if kind in ("in", "gate"):
                                if u == 0:
                                    pe.wait_ge(sem("hT_ready"), at("hT_ready", l, k + 1))
                                hl = (hTh[:, k, :], hTl[:, k, :])
                            elif kind == "out":
                                if half == 0:
                                    pe.wait_ge(sem("mT_ready"), at("mT_ready", l, k + 1))
                                hl = (mT[:, 0, k, :], mT[:, 1, k, :])
                            elif which == "a":
                                hl = (yaT[:, 0, k, :], yaT[:, 1, k, :])
                            elif which == "c":
                                hl = (ycT[:, 0, k, :], ycT[:, 1, k, :])
                            else:
                                if half == 0:
                                    pe.wait_ge(sem("yb_ready"), at("yb_ready", l, k + 1))
                                hl = (ybT[:, k, 0, :], ybT[:, k, 1, :])
                            if which == "a" and half == 0 and kind == "br" and k == 0:
                                pe.wait_ge(sem("ya_ready"), at("ya_ready", l, 4))
                            if which == "c" and half == 0 and kind == "br" and k == 0:
                                pe.wait_ge(sem("yc_ready"), at("yc_ready", l, 4))
                            for t in range(NT):
                                c = slice(t * P, (t + 1) * P)
                                last = mm3(ps[:, base + t, :], (hl[0][:, c], hl[1][:, c]),
                                           (wh[:, p % RING, i, :], wl[:, p % RING, i, :]),
                                           start=k == 0, stop=k == 2 * pairs - 1)
                        last.then_inc(sem("pair_used"), 1)
                        p += 1
                        yield

            stream = dense()

            def pump(n):
                for _ in range(n):
                    next(stream)

            pump(4 * 4)
            pe.wait_ge(sem("small_in"), at("small_in", l, 16 * 4))
            for i in range(2):
                out = aux_start(R_WS + i)
                for g in range(4):
                    last = transpose(out[:, g * P:(g + 1) * P], ws[:, 4 * i + g, :])
                last.then_inc(sem("aux_ready"), 1)
            pump(2)
            for i in range(4):
                out = aux_start(R_SV + i)
                if i == 0:
                    pe.wait_ge(sem("vn_done"), at("vn_done", l, 1))
                for j in range(2):
                    g = 2 * i + j
                    last = pe.matmul(out[:, j * 192:(j + 1) * 192].rearrange("p (t c) -> p t c", t=NT),
                                     wsT[:, g, :], uv[:, :, W + g * 64:W + (g + 1) * 64],
                                     start=True, stop=True)
                last.then_inc(sem("aux_ready"), 1)
            pump(2)
            for i in range(4):
                out = aux_start(R_YA + i)
                if i == 0:
                    pe.wait_ge(sem("ya_tok"), at("ya_tok", l, 1))
                for t in range(NT):
                    last = transpose(out[:, t * P:(t + 1) * P], uv[:, t, i * P:(i + 1) * P])
                last.then_inc(sem("aux_ready"), 1)
            pump(2)
            pe.wait_ge(sem("dft_in"), at("dft_in", l, 48))
            for g in range(4):
                c = slice(g * P, (g + 1) * P)
                out = aux_start(R_DFT + 3 * g)
                for t in range(2):
                    last = pe.matmul(out, f_in[:, 1 + t, c], dft_lat[:, t, :, :].rearrange("p s n -> p (s n)"),
                                     start=t == 0, stop=t == 1)
                last.then_inc(sem("aux_ready"), 1)
                out = aux_start(R_DFT + 3 * g + 1)
                pe.matmul(out[:, 0:256], f_in[:, 0, c], dft_pr[:, :, :].rearrange("p s n -> p (s n)"),
                          start=True, stop=True).then_inc(sem("aux_ready"), 1)
                pump(1)
                out = aux_start(R_DFT + 3 * g + 2)
                pe.wait_ge(sem("dft_copied"), at("dft_copied", l, g + 1))
                for s in range(2):
                    last = pe.matmul(out[:, 0:T], dft_ch[:, s, :], spec[:, s, :], start=s == 0, stop=s == 1)
                last.then_inc(sem("aux_ready"), 1)
            pump(PAIRS_W_IN - 4 * 4 - 6 - 4)

            pe.wait_ge(sem("evac_act"), at("evac_act", l, N_IN))
            pe.wait_ge(sem("aux_free"), at("aux_free", l, AUX))
            pe.wait_ge(sem("cache_in"), at("cache_in", l, 32))
            pe.wait_ge(sem("qk_normed"), at("qk_normed", l, 1))
            for h in range(HEADS):
                if h:
                    pe.wait_ge(sem("exp_done"), at("exp_done", l, 3 * h))
                for t in range(NT):
                    transpose(ps[:, 6, t * P:(t + 1) * P], qk[:, h, 0, t, :])
                transpose(ps[:, 7, 0:P], kc[:, h, :])
                for t in range(NT):
                    last = transpose(ps[:, 7, (3 if t == 0 else t) * P:(4 if t == 0 else t + 1) * P],
                                     qk[:, h, 1, t, :])
                last.then_inc(sem("qkT_acc"), 1)
                pump(1)
                pe.wait_ge(sem("qT_done"), at("qT_done", l, h + 1))
                pe.wait_ge(sem("kT_done"), at("kT_done", l, h + 1))
                if h:
                    pe.wait_ge(sem("o_copied"), at("o_copied", l, h))
                for t in (1, 0, 2):
                    for m in range(MAPS):
                        rows = slice(m * DQ, (m + 1) * DQ)
                        if t == 0:
                            out, keys = ps[:, 4 + m, T:4 * P], kT[rows, 3 * P:4 * P]
                        else:
                            out, keys = ps[:, (4 if t == 1 else 6) + m, 0:T], kT[rows, 0:T]
                        last = pe.matmul(out, qT[rows, t * P:(t + 1) * P], keys, start=True, stop=True)
                    if t != 1:
                        last.then_inc(sem("score_acc"), 1)
                pump(1)
                pe.wait_ge(sem("diff_done"), at("diff_done", l, 3 * h + 2))
                for j in range(3):
                    transpose(ps[:, 3, j * P:(j + 1) * P], e12[:, 0, 0, j * P:(j + 1) * P])
                transpose(ps[:, 3, 3 * P:4 * P], e0[:, 0, :]).then_inc(sem("aT_acc"), 1)
                pe.wait_ge(sem("diff_done"), at("diff_done", l, 3 * h + 3))
                for j in range(3):
                    last = transpose(ps[:, 5, j * P:(j + 1) * P], e12[:, 1, 0, j * P:(j + 1) * P])
                last.then_inc(sem("aT_acc"), 1)
                pump(1)
                pe.wait_ge(sem("aT_copied"), at("aT_copied", l, 2 * h + 2))
                v = slice(h * P, (h + 1) * P)
                pe.matmul(ps[:, 4, 0:P], aT[:, 3, :], vv[:, 0, v], start=True, stop=True)
                for t in (1, 2):
                    for j in range(3):
                        vals = vc[:, h, :] if j == 0 else vv[:, j, v]
                        last = pe.matmul(ps[:, 4, t * P:(t + 1) * P], aT[:, (0 if t == 1 else 4) + j, :], vals,
                                         start=j == 0, stop=j == 2)
                last.then_inc(sem("o_acc"), 1)

            pump(4)
            for h in range(HEADS):
                if h < 2:
                    pe.wait_ge(sem("exp_done"), at("exp_done", l, 3 * HEADS))
                    out = ps[:, 6 + (R_YB + h) % 2, :]
                else:
                    out = aux_start(R_YB + h)
                if h == 0:
                    pe.wait_ge(sem("o_normed"), at("o_normed", l, 1))
                for t in range(NT):
                    last = transpose(out[:, t * P:(t + 1) * P], qk[:, h, 0, t, :])
                last.then_inc(sem("aux_ready"), 1)
            pump(4)
            pump(2)
            for k in range(KD):
                if k == KD // 2:
                    pump(8)
                out = aux_start(R_MERGED + k)
                pe.wait_ge(sem("merged_done"), at("merged_done", l, 5 if k < 4 else 6))
                for t in range(NT):
                    last = transpose(out[:, t * P:(t + 1) * P], merged[:, t, k * P:(k + 1) * P])
                last.then_inc(sem("aux_ready"), 1)
            pump(PAIRS_OUT - 2)

            pe.wait_ge(sem("evac_dve"), at("evac_dve", l, 7))
            mods = modulation(beside_router(l), COLS_IN[l + 1])

            def pump_mod(n):
                for _ in range(n):
                    next(mods, None)

            assert MOD_FIRST <= PAIRS_BLOCK + 2
            norm_transposes(1, R_NORM2)
            pe.wait_ge(sem("evac_dve"), at("evac_dve", l, 8))
            pump_mod(1)
            pe.wait_ge(sem("rw_ready"), 1)
            out = aux_start(R_LOGITS)
            pe.wait_ge(sem("hT_ready"), at("hT_ready", l, 2 * KD))
            for t in range(NT):
                c = slice(t * P, (t + 1) * P)
                for k in range(KD):
                    last = mm3(out[:, t * NE:(t + 1) * NE], (hTh[:, k, c], hTl[:, k, c]),
                               (rwh[:, k, :], rwl[:, k, :]), start=k == 0, stop=k == KD - 1)
            last.then_inc(sem("aux_ready"), 1)
            r = R_BACK
            for t in range(NT):
                for half in range(2):
                    for s, src in enumerate((hTh, hTl)):
                        pump_mod(1)
                        out = aux_start(r)
                        for k in range(4):
                            last = transpose(out[:, k * P:(k + 1) * P],
                                             src[:, 4 * half + k, t * P:(t + 1) * P].bitcast(F32))
                        last.then_inc(sem("aux_ready"), 1)
                        r += 1
            pump_mod(MOD_SLOTS - MOD_FIRST - 1 - 4 * NT)
            def gather(pair, half, bank, steps=(0, 1, 2, 3)):
                for i in steps:
                    k = 4 * half + i
                    o = ps[:, bank + i // 2, (i % 2) * 2 * P:(i % 2 + 1) * 2 * P]
                    for s in range(2):
                        for t in range(NT):
                            last = pe.matmul(o, h2[:, s, t, k * P:(k + 1) * P], pick[:, t, pair, :],
                                             start=s == 0 and t == 0, stop=s == 1 and t == NT - 1)
                if steps[-1] == 3:
                    last.then_inc(sem("X_acc"), 1)

            def turn_pick(pair, odd):
                for t in range(NT):
                    last = transpose(ps[:, 6, t * P:(t + 1) * P], pick[:, t, pair, odd * P:(odd + 1) * P].bitcast(F32))
                last.then_inc(sem("PT_acc"), 1)

            def combine(e, odd, c, after_first=False):
                t, half = c // 2, c % 2
                if c >= 2:
                    pe.wait_ge(sem("comb_done"), at("comb_done", l, c - 1) + e * 6)
                elif c == 1 and not after_first:
                    pe.wait_ge(sem("comb_done"), at("comb_done", l, 0) + e * 6)
                for s in range(2):
                    last = pe.matmul(ps[:, 6 + c % 2, :], pickT[:, odd, t, :],
                                     oe[:, s, half * W:(half + 1) * W], start=s == 0, stop=s == 1)
                last.then_inc(sem("comb_acc"), 1)

            def expert(e, odd, pair, first=False, last_pair=False, last_one=False):
                rows = slice(odd * P, (odd + 1) * P)
                if not odd:
                    pe.wait_ge(sem("xe_ready"), at("xe_ready", l, 2) + e)
                for q in range(8):
                    name, value = lo_at(l, e, q)
                    pe.wait_ge(sem(name), value)
                    for i in range(2):
                        k = 2 * (q % 4) + i
                        last = mm3(ps[:, 2 + q // 4, :], (xeT[:, 0, k, rows], xeT[:, 1, k, rows]),
                                   (wxh[:, q % RING_MOE, i, :], wxl[:, q % RING_MOE, i, :]), start=k == 0, stop=k == KD - 1)
                    last.then_inc(sem("pair_used"), 1)
                    if q >= 2 and not first:
                        if q == 2:
                            pe.wait_ge(sem("out_ready"), at("out_ready", l, 0) + e)
                            pe.wait_ge(sem("PT_done"), at("PT_done", l, 1) + e)
                        combine(e - 1, 1 - odd, q - 2, after_first=isinstance(e, int) and e == 1)
                if not odd and not last_pair:
                    pe.wait_ge(sem("pick_ready"), at("pick_ready", l, 4) + e)
                    gather(1 - pair, 0, 0, steps=(0, 1))
                pe.wait_ge(sem("a_done"), at("a_done", l, 1) + e)
                for k in range(4):
                    last = transpose(ps[:, 4, k * P:(k + 1) * P], ae[:, k * P:(k + 1) * P])
                last.then_inc(sem("eT_acc"), 1)
                if not last_pair:
                    if odd:
                        gather(1 - pair, 1, 2)
                    else:
                        gather(1 - pair, 0, 0, steps=(2, 3))
                if not last_one:
                    if first:
                        pe.wait_ge(sem("PT_done"), at("PT_done", l, 1))
                    else:
                        pe.wait_ge(sem("comb_done"), (e - 1) * 6 + at("comb_done", l, 5))
                    turn_pick(1 - pair if odd else pair, 1 - odd)
                pe.wait_ge(sem("eT_ready"), at("eT_ready", l, 1) + e)
                for q in range(8, PAIRS_EXPERT):
                    name, value = lo_at(l, e, q)
                    pe.wait_ge(sem(name), value)
                    for i in range(2):
                        k = 2 * (q % 2) + i
                        last = mm3(ps[:, 4 + (q - 8) // 2, :], (eaT[:, 0, k, :], eaT[:, 1, k, :]),
                                   (wxh[:, q % RING_MOE, i, :], wxl[:, q % RING_MOE, i, :]), start=k == 0, stop=k == 3)
                    last.then_inc(sem("pair_used"), 1)

            out = aux_start(R_SLOTS)
            pe.wait_ge(sem("mask_done"), at("mask_done", l, 1))
            for t in range(NT):
                for s in range(t + 1):
                    pe.matmul(out[:, t * NE:(t + 1) * NE], tri[:, 0 if s == t else 1, :], mask[:, s, :],
                              start=s == 0, stop=s == t)
            for s in range(NT):
                last = pe.matmul(out[:, NT * NE:(NT + 1) * NE], tri[:, 1, :], mask[:, s, :],
                                 start=s == 0, stop=s == NT - 1)
            last.then_inc(sem("aux_ready"), 1)

            pump_mod(MOD_GATHER - MOD_SLOTS)
            pe.wait_ge(sem("aux_free"), at("aux_free", l, AUX_ROUNDS))
            pe.wait_ge(sem("evac_dve"), at("evac_dve", l, 8))
            pe.wait_ge(sem("pick_ready"), at("pick_ready", l, 2))
            gather(0, 0, 0)
            turn_pick(0, 0)
            pump_mod(MOD_BETWEEN)
            pe.wait_ge(sem("xe_ready"), at("xe_ready", l, 1))
            gather(0, 1, 0)
            pump_mod(PAIRS_BLOCK * MOD_BLOCKS)
            pe.wait_ge(sem("gate_done"), gates[0])
            if l + 1 < DEPTH:
                pe.wait_ge(sem("col_ready"), at("col_ready", l + 1, 1))
            expert_loop(pe, expert)
            pe.wait_ge(sem("out_ready"), at("out_ready", l, NE))
            for c in range(6):
                combine(NE - 1, (NE - 1) % 2, c)

            def turn(e, b):
                over_dve = sem(f"over_dve{l}")
                over_pe = sem(f"over_pe{l}")

                def wait_dve(k):
                    pe.wait_ge(over_dve, over_at("dve", e, b, k))

                def chunk(i):
                    wait_dve(OVER_DVE[f"c{i}"])
                    for k in range(4):
                        s = (xeT1 if i < 4 else eaT)
                        j = k + (4 * (i % 2) if i < 4 else 0)
                        last = mm3(ps[:, (2, 2, 3, 3, 4, 5)[i], :], (s[:, 0, j, :], s[:, 1, j, :]),
                                   (wh[:, k // 2, k % 2, :], wl[:, k // 2, k % 2, :]),
                                   start=k == 0 and i in (0, 2, 4, 5), stop=k == 3 and i in (1, 3, 4, 5))
                    last.then_inc(over_pe, 1)

                wait_dve(OVER_DVE["pick"])
                for k in range(KD):
                    o = ps[:, k // 4, (k % 4) * P:(k % 4 + 1) * P]
                    for s in range(2):
                        for t in range(NT):
                            pe.matmul(o, h2[:, s, t, k * P:(k + 1) * P], pick1[:, t, :],
                                      start=s == 0 and t == 0, stop=s == 1 and t == NT - 1)
                for t in range(NT):
                    last = transpose(ps[:, 6, t * P:(t + 1) * P], pick1[:, t, :].bitcast(F32))
                last.then_inc(over_pe, 1)
                for i in range(4):
                    chunk(i)
                wait_dve(OVER_DVE["a"])
                for k in range(4):
                    last = transpose(ps[:, 7, k * P:(k + 1) * P], ae[:, k * P:(k + 1) * P])
                last.then_inc(over_pe, 1)
                chunk(4)
                chunk(5)
                for c in range(6):
                    wait_dve(OVER_DVE["out_lo"] if c < 2 else OVER_DVE["part"] + c - 2)
                    for s in range(2):
                        last = pe.matmul(ps[:, 6 + c % 2, :], pickT[:, 0, c // 2, :],
                                         oe[:, s, (c % 2) * W:(c % 2 + 1) * W], start=s == 0, stop=s == 1)
                    last.then_inc(over_pe, 1)

            second_pass(pe, l, turn)

    def scalar_program(act):
        chain = Chain(act, "act_chain")
        link = chain.link

        def hi(p):
            c = p // 2
            act.wait_ge(landed[c % RAW], landed_at(c))
            if p >= RING:
                act.wait_ge(sem("pair_used"), p - RING + 1)
            s = 2 * (p % 2)
            act.activation(wh[:, p % RING, :, :], raw[:, c % RAW, s:s + 2, :], ACT.Copy
                           ).then_inc(sem("hi_done"), 1)

        def load_cols(lc, rest=None):
            if lc is not None:
                for dst, src in (
                        (srow[0:8, :], io["norm1_w"][bass.ds(lc, 1), :].rearrange("a (k p) -> (a k) p", p=P)),
                        (srow[8:16, :], io["norm2_w"][bass.ds(lc, 1), :].rearrange("a (k p) -> (a k) p", p=P)),
                        (srow[16:24, :], io["a_b_s"][bass.ds(lc, 1), :, :].rearrange("a g p -> (a g) p")),
                        (srow[24:25, :], io["subln_w"][bass.ds(lc, 1), :]),
                        (modrow[4:5, 0:MOD_EARLY, :],
                         io["b_mod"][bass.ds(lc, 1), 0:MOD_EARLY * W].rearrange("a (n w) -> a n w", w=W))):
                    act.dma_start(dst, src).then_inc(sem("cols_in"), 16)
            if rest is not None:
                act.dma_start(modrow[4:5, MOD_EARLY:MOD_BLOCKS, :],
                              io["b_mod"][bass.ds(rest, 1), MOD_EARLY * W:].rearrange("a (n w) -> a n w", w=W)
                              ).then_inc(sem("cols_in"), 16)

        def modulation(blocks):
            def row(l, n):
                first, number = block_pair(l, n)
                act.wait_ge(sem("pair_used"), first + PAIRS_BLOCK)
                act.activation(modrow[0:4, n, :], ps[0:4, 3 + n % 2, :], ACT.Copy).then_inc(sem("modrow_done"), 1)

            def gate(n, g):
                gates[0] += 1
                act.wait_ge(sem("gate_acc"), gates[0])
                act.activation(gbc[:, 0 if n < MOD_EARLY else 1, g, (n % 2) * W:(n % 2 + 1) * W],
                               ps[:, 2, :], ACT.Copy).then_inc(sem("gate_done"), 1)

            for i, (l, n) in enumerate(blocks):
                for q in range(PAIRS_BLOCK):
                    hi(block_pair(l, n)[0] + q)
                    if q < 2 and i >= 2 and blocks[i - 2][1] in GATES:
                        gate(blocks[i - 2][1], q)
                    if q == 1 and i:
                        row(*blocks[i - 1])
                    yield
            before, last = blocks[-2][1], blocks[-1][1]
            yield
            if before in GATES:
                gate(before, 0)
            yield
            if before in GATES:
                gate(before, 1)
            row(*blocks[-1])
            yield
            if last in GATES:
                gate(last, 0)
                gate(last, 1)

        gates = [0]
        GATES = (4, 5, 10, 11)


        def root(name, l, k, out, in_):
            act.wait_ge(sem(name[0]), at(name[0], l, k))
            act.activation(out, in_, ACT.Sqrt).then_inc(sem(name[1]), 1)

        for dst, src in first_loads():
            act.dma_start(dst, src).then_inc(sem("first_in"), 16)
        load_cols(0)
        for dst, src in const_loads():
            act.dma_start(dst, src).then_inc(sem("const_in"), 16)
        act.wait_ge(sem("crow_acc"), 1)
        act.activation(csil[:, :], ps[:, 0, 0:16], ACT.Silu).then_inc(sem("csil_done"), 1)
        act.wait_ge(sem("csil_done"), 1)
        for g in range(2):
            ins = act.activation(cs[:, :, g], csil[:, 8 - 8 * g:16 - 8 * g], ACT.Copy)
        ins.then_inc(sem("cs_hi"), 1)
        mods = modulation(early_blocks(0))

        for l in range(DEPTH):
            if l == 0:
                for _ in range(MOD_STATS):
                    next(mods)
                act.wait_ge(sem("x_in"), 16 * NT)

            def norm_stats(which, wait=None):
                for t in range(NT):
                    if t:
                        act.wait_ge(sem("act_junk"), junk_n[0])
                    if which:
                        act.wait_ge(sem("x_mid"), at("x_mid", l, t + 1))
                    elif l:
                        act.wait_ge(sem("x_ready"), at("x_ready", l - 1, t + 1))
                    ins = act.activation(junk[:, :], x[:, t, :], ACT.Square, accum_out=st[:, t:t + 1])
                    if t < NT - 1:
                        junk_n[0] += 1
                        ins.then_inc(sem("act_junk"), 1)
                    else:
                        ins.then_inc(sem("sumsq"), 1)
                act.wait_ge(sem("meansq"), at("meansq", l, which + 1))
                act.activation(st[:, 6:9], st[:, 3:6], ACT.Sqrt).then_inc(sem("root"), 1)

            norm_stats(0)
            if l == 0:
                for _ in mods:
                    pass
                act.wait_ge(sem("const_in"), 16 * N_CONST)
                act.activation(rwh[:, :, :], rw[:, :, :], ACT.Copy).then_inc(sem("rw_hi"), 1)
            for i in range(RING):
                hi(DENSE0[l] + i)

            def split_hi(out, r, name, k, scale=None):
                act.wait_ge(sem("aux_ready"), at("aux_ready", l, r + 1))
                kw = {} if scale is None else dict(scale=scale)
                act.activation(out, ps[:, 6 + r % 2, 0:T], ACT.Copy if scale is None else ACT.Identity, **kw
                               ).then_inc(sem(name), 1)

            def norm_hi(which):
                for k in range(KD):
                    n = which * KD + k + 1
                    act.wait_ge(sem("full_done"), at("full_done", l, n))
                    act.activation(hTh[:, k, :], full[:, k % 2, :], ACT.Copy).then_inc(sem("hT_hi"), 1)

            norm_hi(0)
            act.wait_ge(sem("x_ready"), at("x_ready", l, 0))
            rows = [(anorm[:, :], io["a_norm_w"][bass.ds(l, 1), :].broadcast_to([P, W])),
                    (lamv[:, :, :], io["lambda_qk"][bass.ds(l, 1), :, :].broadcast_to([P, 4, DQ])),
                    (ws[:, :, :], io["a_w_s"][bass.ds(l, 1), :, :, :].rearrange("a g p q -> p (a g) q")),
                    (rope0[:, :, :, :], io["t_rope"])]
            for dst, src in rows:
                act.dma_start(dst, src).then_inc(sem("small_in"), 16)
            for i, name in enumerate(("q_norm_w", "k_norm_w")):
                for m in range(MAPS):
                    act.dma_start(qkn[:, i, m, :], io[name][bass.ds(l, 1), :].broadcast_to([P, DQ])
                                  ).then_inc(sem("qkn_in"), 16)
            for dst, src in ((dft_lat, io["t_dft_lat"]), (dft_pr, io["t_dft_pr"]), (dft_ch, io["t_dft_ch"])):
                act.dma_start(dst[tuple([slice(None)] * len(dst.shape))], src).then_inc(sem("dft_in"), 16)

            done = [DENSE0[l] + RING]

            def evac(u):
                kind, which, half, _ = USES[u]
                act.wait_ge(sem("pair_used"), use_end(l, u))
                beside = FIRST_BR <= u < FIRST_BR + 8
                base = 0 if beside else 3 * (u % 2)
                src = ps[:, base:base + NT, :]
                if kind == "gate":
                    n = (u - FIRST_BR) // 2
                    if n:
                        act.wait_ge(sem("merged_done"), at("merged_done", l, n))
                    act.activation(gs[:, :, :], src, ACT.Sigmoid).then_inc(sem("evac_act"), 1)
                elif which == 0:
                    act.activation(uv[:, :, 0:W], src, ACT.Gelu_apprx_tanh).then_inc(sem("evac_act"), 1)
                elif which == 1:
                    act.activation(uv[:, :, W:2 * W], src, ACT.Gelu_apprx_tanh).then_inc(sem("evac_act"), 1)
                elif which == 8:
                    act.activation(f_in[:, :, :], src, ACT.Copy).then_inc(sem("evac_act"), 1)
                elif which < 6:
                    s, h0 = (which - 2) // 2, 4 * (which % 2)
                    for t in range(NT):
                        ins = act.activation(qk[:, h0:h0 + 4, s, t, :],
                                             ps[:, base + t, :].rearrange("p (h d) -> p h d", h=4), ACT.Copy)
                    ins.then_inc(sem("evac_act"), 1)
                else:
                    c = (which - 6) * W
                    act.activation(vv[:, :, c:c + W], src, ACT.Copy).then_inc(sem("evac_act"), 1)

            base = DENSE0[l]

            def hi_to(n):
                while done[0] < base + n:
                    hi(done[0])
                    done[0] += 1

            hi_to(6)
            evac(0)
            hi_to(10)
            evac(1)
            for t in range(NT):
                if t == 0:
                    act.wait_ge(sem("evac_act"), at("evac_act", l, 2))
                else:
                    act.wait_ge(sem("act_junk"), junk_n[0])
                ins = act.activation(junk[:, 0:W], uv[:, t, W:2 * W], ACT.Square, accum_out=st[:, t:t + 1])
                if t < NT - 1:
                    ins.then_inc(sem("act_junk"), 1)
                    junk_n[0] += 1
                else:
                    ins.then_inc(sem("v_sumsq"), 1)
            act.wait_ge(sem("v_meansq"), at("v_meansq", l, 1))
            act.activation(st[:, 6:9], st[:, 3:6], ACT.Sqrt).then_inc(sem("v_root"), 1)
            hi_to(14)
            evac(2)
            hi_to(15)
            act.wait_ge(sem("lam_dot"), at("lam_dot", l, 1))
            act.activation(lam[:, 2:4], lam[:, 0:2], ACT.Exp).then_inc(sem("lam_exp"), 1)
            hi_to(18)
            evac(3)
            hi_to(23)
            for i in range(4):
                split_hi(yaT[:, 0, i, :], R_YA + i, "ya_hi", i)
            hi_to(25)
            evac(4)
            for g in range(4):
                hi_to(26 + g)
                split_hi(ycT[:, 0, g, :], R_DFT + 3 * g + 2, "yc_hi", g)
                if g == 1:
                    evac(5)
            act.wait_ge(sem("yc_hi"), at("yc_hi", l, 4))
            for dst, name in ((kc, "cache_k"), (vc, "cache_v")):
                act.dma_start(dst[:, :, :], io[name][0, bass.ds(l, 1), :, :, :].rearrange("a s h d -> s (a h) d")
                              ).then_inc(sem("cache_in"), 16)

            def squares(s, t):
                i = s * NT + t
                if i:
                    act.wait_ge(sem("qk_summed"), at("qk_summed", l, i))
                else:
                    act.wait_ge(sem("dft_copied"), at("dft_copied", l, 4))
                if t == 0:
                    act.wait_ge(sem("evac_act"), at("evac_act", l, 5 + 2 * s))
                act.activation(qsq[:, :].rearrange("p (h d) -> p h d", h=HEADS), qk[:, :, s, t, :], ACT.Square
                               ).then_inc(sem("qk_sumsq"), 1)

            def roots(s):
                act.wait_ge(sem("qk_meansq"), at("qk_meansq", l, s + 1))
                act.activation(qst[:, s * NT:(s + 1) * NT, :], qst[:, s * NT:(s + 1) * NT, :], ACT.Sqrt
                               ).then_inc(sem("qk_root"), 1)

            squares(0, 0)
            hi_to(30)
            squares(0, 1)
            squares(0, 2)
            roots(0)
            hi_to(31)
            evac(6)
            squares(1, 0)
            hi_to(34)
            squares(1, 1)
            evac(7)
            hi_to(35)
            squares(1, 2)
            roots(1)
            hi_to(38)
            evac(N_IN - 1)
            hi_to(39)
            act.wait_ge(sem("evac_act"), at("evac_act", l, N_IN))
            act.dma_start(io["new_v"][0, bass.ds(l, 1), :, :, :].rearrange("a s h d -> s (a h) d"),
                          vv[:, 0, :].rearrange("p (h d) -> p h d", h=HEADS)).then_inc(sem("kv_out"), 16)
            act.wait_ge(sem("qk_normed"), at("qk_normed", l, 1))
            act.dma_start(io["new_k"][0, bass.ds(l, 1), :, :, :].rearrange("a s h d -> s (a h) d"),
                          qk[:, :, 1, 0, :]).then_inc(sem("kv_out"), 16)

            att_done = [0]
            ends = {4: FIRST_BR, 10: FIRST_BR + 2, 16: FIRST_BR + 4, 22: FIRST_BR + 6}
            assert done[0] == DENSE0[l] + PAIRS_W_IN + RING

            def beside(n):
                for _ in range(n):
                    hi(done[0])
                    done[0] += 1
                    att_done[0] += 1
                    if att_done[0] in ends:
                        evac(ends[att_done[0]])

            for h in range(HEADS):
                act.wait_ge(sem("qkT_acc"), at("qkT_acc", l, h + 1))
                act.activation(qT[:, :], ps[:, 6, 0:T], ACT.Copy).then_inc(sem("qT_done"), 1)
                beside(1)
                for i, t in enumerate((1, 0, 2)):
                    act.wait_ge(sem("score_max"), at("score_max", l, 3 * h + max(i, 1) + 1))
                    for m in range(MAPS):
                        if t == 0:
                            out, src = e0[:, m, :], ps[:, 4 + m, T:4 * P]
                        else:
                            out, src = e12[:, t - 1, m, :], ps[:, (4 if t == 1 else 6) + m, 0:T]
                        ins = act.activation(out, src, ACT.Exp, bias=nmx[:, t, m:m + 1], scale=DQ ** -0.5,
                                             accum_out=es[:, t, m:m + 1])
                    ins.then_inc(sem("exp_done"), 1)
                beside(1)
                for i in range(2):
                    act.wait_ge(sem("aT_acc"), at("aT_acc", l, 2 * h + i + 1))
                    n = 4 if i == 0 else 3
                    act.activation(aT[:, 4 * i:4 * i + n, :],
                                   ps[:, 3 + 2 * i, 0:n * P].rearrange("p (k n) -> p k n", k=n), ACT.Copy
                                   ).then_inc(sem("aT_copied"), 1)
                beside(1)
            act.wait_ge(sem("o_copied"), at("o_copied", l, HEADS))
            for t in range(NT):
                if t:
                    act.wait_ge(sem("o_summed"), at("o_summed", l, t))
                act.activation(o_sq[:, :].rearrange("p (h d) -> p h d", h=HEADS), qk[:, :, 0, t, :], ACT.Square
                               ).then_inc(sem("o_sq"), 1)
                if t == 0:
                    hi_to(PAIRS_W_IN + ATT_PAIRS + 4)
            act.wait_ge(sem("o_meansq"), at("o_meansq", l, 1))
            act.activation(qst[:, 0:3, 0:8], qst[:, 0:3, 0:8], ACT.Sqrt).then_inc(sem("o_root"), 1)
            n = PAIRS_W_IN + ATT_PAIRS + 4
            hi_to(n + 3)
            for h in range(HEADS):
                split_hi(ybT[:, h, 0, :], R_YB + h, "yb_hi", h, scale=subc[:, 0:1])
            evac(FIRST_BR + 8)
            hi_to(n + 9)
            for k in range(4):
                split_hi(mT[:, 0, k, :], R_MERGED + k, "mT_hi", k)
            hi_to(n + 10)
            evac(FIRST_BR + 10)
            hi_to(n + 17)
            for k in range(4, KD):
                split_hi(mT[:, 0, k, :], R_MERGED + k, "mT_hi", k)
            hi_to(PAIRS_DENSE)
            assert done[0] == MOD0[l]

            mods = modulation(beside_router(l))
            for i in range(RING):
                next(mods, None)
            norm_stats(1)
            load_cols(l + 1 if l + 1 < DEPTH else None, l)
            for i in range(MOD_FIRST):
                next(mods, None)
            norm_hi(1)
            act.wait_ge(sem("aux_ready"), at("aux_ready", l, R_LOGITS + 1))
            act.activation(s_r[:, :, :].rearrange("p t e -> p (t e)"), ps[:, 6 + R_LOGITS % 2, 0:NT * NE], ACT.Sigmoid
                           ).then_inc(sem("score_done"), 1)
            next(mods, None)
            act.wait_ge(sem("score_done"), at("score_done", l, 1))
            act.sem_inc(sem("aux_free"), 1)
            for i in range(4 * NT):
                r = R_BACK + i
                next(mods, None)
                act.wait_ge(sem("aux_ready"), at("aux_ready", l, r + 1))
                act.activation(h2[:, i % 2, i // 4, (i // 2 % 2) * W:(i // 2 % 2 + 1) * W], ps[:, 6 + r % 2, :], ACT.Copy
                               ).then_inc(sem("aux_free"), 1)
            for i in range(MOD_GATHER - MOD_FIRST - 4 * NT):
                next(mods, None)
            def expert_hi(e, q):
                place, value = expert_chunk(l, e, q // 2)
                act.wait_ge(landed[place], value)
                if isinstance(e, int) and e == 0 and q < RING:
                    act.wait_ge(sem("pair_used"), MOE0[l] - (MOE0[l] - 1 - q) % RING)
                elif not (isinstance(e, int) and e == 0 and q < RING_MOE):
                    act.wait_ge(sem("pair_used"), used_at(l, e, q - RING_MOE))
                s = 2 * (q % 2)
                act.activation(wxh[:, q % RING_MOE, :, :], raw[:, place, s:s + 2, :], ACT.Copy
                               ).then_inc(sem("hi_done"), 1)

            def gathered(count, half, bank):
                act.wait_ge(sem("X_acc"), count)
                act.activation(xeT[:, 0, 4 * half:4 * half + 4, :],
                               ps[:, bank:bank + 2, :].rearrange("p b (k n) -> p (b k) n", k=2), ACT.Copy
                               ).then_inc(sem("xe_hi"), 1)

            def turned_pick(e, odd):
                act.wait_ge(sem("PT_acc"), at("PT_acc", l, 1) + e)
                act.activation(pickT[:, odd, :, :], ps[:, 6, 0:T].rearrange("p (t n) -> p t n", t=NT), ACT.Copy
                               ).then_inc(sem("PT_done"), 1)

            def expert(e, odd, pair, first=False, last_pair=False, last_one=False):
                for q in range(4, 9):
                    expert_hi(e, q)
                act.wait_ge(sem("pair_used"), used_at(l, e, 3))
                act.activation(sg[:, :], ps[:, 2, :], ACT.Silu).then_inc(sem("silu_done"), 1)
                for q in range(9, 12 if last_one else 13):
                    expert_hi(e, q)
                act.wait_ge(sem("eT_acc"), at("eT_acc", l, 1) + e)
                act.activation(eaT[:, 0, :, :], ps[:, 4, :].rearrange("p (k n) -> p k n", k=4), ACT.Copy
                               ).then_inc(sem("eT_hi"), 1)
                if odd and not last_pair:
                    act.wait_ge(sem("pair_used"), used_at(l, e, 7))
                    gathered(at("X_acc", l, 2) + e, 0, 0)
                    gathered(at("X_acc", l, 3) + e, 1, 2)
                if not last_one:
                    turned_pick(e + 1, 1 - odd)
                    for q in range(13, 16):
                        expert_hi(e, q)
                act.wait_ge(sem("pair_used"), used_at(l, e, PAIRS_EXPERT - 1))
                act.activation(oe[:, 0, :].rearrange("p (b n) -> p b n", b=2), ps[:, 4:6, :], ACT.Copy
                               ).then_inc(sem("out_hi"), 1)

            gathered(at("X_acc", l, 1), 0, 0)
            turned_pick(0, 0)
            for i in range(MOD_BETWEEN):
                next(mods, None)
            gathered(at("X_acc", l, 2), 1, 0)
            for _ in mods:
                pass
            for q in range(RING):
                expert_hi(0, q)
            expert_hi(0, 3)
            expert_loop(act, expert)

            def turn(e, b):
                over_act = sem(f"over_act{l}")

                def wait_pe(k):
                    act.wait_ge(sem(f"over_pe{l}"), over_at("pe", e, b, k))

                def chunk(i):
                    act.wait_ge(sem(f"over_dma{l}"), over_at("dma", e, b, 16 * (i + 1)))
                    wait_pe(OVER_PE["gathered"] if i == 0 else OVER_PE[f"c{i - 1}"])
                    act.activation(wh[:, 0:2, :, :].rearrange("p r i n -> p (r i) n"), raw[:, 0, :, :], ACT.Copy
                                   ).then_inc(over_act, 1)

                wait_pe(OVER_PE["gathered"])
                act.activation(xeT1[:, 0, :, :], ps[:, 0:2, :].rearrange("p b (k n) -> p (b k) n", k=4), ACT.Copy
                               ).then_inc(over_act, 1)
                for i in range(4):
                    chunk(i)
                wait_pe(OVER_PE["c1"])
                act.activation(sg[:, :], ps[:, 2, :], ACT.Silu).then_inc(over_act, 1)
                wait_pe(OVER_PE["turned"])
                act.activation(eaT[:, 0, :, :], ps[:, 7, :].rearrange("p (k n) -> p k n", k=4), ACT.Copy
                               ).then_inc(over_act, 1)
                chunk(4)
                chunk(5)
                wait_pe(OVER_PE["c5"])
                act.activation(oe[:, 0, :].rearrange("p (b n) -> p b n", b=2), ps[:, 4:6, :], ACT.Copy
                               ).then_inc(over_act, 1)

            second_pass(act, l, turn)
        act.wait_ge(sem("kv_out"), at("kv_out", DEPTH - 1, 32))

    def gpsimd_program(pool):
        def low_parts(first, end):
            for p in range(first, end):
                if LOW[p][0] == "lo_pool":
                    s = 2 * (p % 2)
                    pool.wait_ge(sem("hi_done"), p + 1)
                    pool.tensor_tensor(wl[:, p % RING, :, :], raw[:, p // 2 % RAW, s:s + 2, :],
                                       wh[:, p % RING, :, :].bitcast(F32), ALU.subtract).then_inc(sem("lo_pool"), 1)

        low_parts(0, DENSE0[0])
        gates = 4
        for l in range(DEPTH):
            low_parts(DENSE0[l], MOE0[l])
            gates += 2 * sum(1 for _, n in beside_router(l) if n in (4, 5, 10, 11))
            pool.wait_ge(sem("gate_acc"), gates)
            pool.memset(y[:, :, :], 0.0).then_inc(sem("y_zero"), 1)

            def expert(e, odd, pair, first=False, last_pair=False, last_one=False):
                for q in POOL_Q:
                    pool.wait_ge(sem("hi_done"), used_at(l, e, q))
                    pool.tensor_tensor(wxl[:, q % RING_MOE, :, :], raw[:, expert_chunk(l, 0, q // 2)[0], 2 * (q % 2):2 * (q % 2) + 2, :],
                                       wxh[:, q % RING_MOE, :, :].bitcast(F32), ALU.subtract).then_inc(sem("lo_pool"), 1)

            expert_loop(pool, expert)

    def vector_program(dve):
        chain = Chain(dve, "dve_chain")
        link = chain.link
        dve.sem_inc(sem("x_ready"), 1)

        def lo(p):
            if LOW[p][0] != "lo_dve":
                return
            s = 2 * (p % 2)
            dve.wait_ge(sem("hi_done"), p + 1)
            dve.tensor_tensor(wl[:, p % RING, :, :], raw[:, p // 2 % RAW, s:s + 2, :],
                              wh[:, p % RING, :, :].bitcast(F32), ALU.subtract).then_inc(sem("lo_dve"), 1)

        dve.wait_ge(sem("cs_hi"), 1)
        for g in range(2):
            ins = dve.tensor_tensor(cs[:, :, 2 + g], csil[:, 8 - 8 * g:16 - 8 * g], cs[:, :, g].bitcast(F32),
                                    ALU.subtract)
        ins.then_inc(sem("cs_ready"), 1)
        for p in range(MOD_STATS):
            lo(p)

        def columns(l):
            dve.wait_ge(sem("mcol_acc"), at("mcol_acc", l, 1))
            link(dve.tensor_copy(scol[:, :], ps[:, 5, 64:89]))
            mc = ps[:, 5, 0:64].rearrange("p (w k g) -> p w k g", w=4, g=2)
            for i in range(2):
                dve.tensor_copy(shf[:, i, :, :], mc[:, 2 * i, :, :])
                dve.scalar_tensor_tensor(scl[:, i, :, :], mc[:, 2 * i + 1, :, :], 1.0,
                                         scol[:, 8 * i:8 * i + 8].unsqueeze(2).to_broadcast([P, KD, 2]),
                                         ALU.add, ALU.mult)
            dve.tensor_scalar(subc[:, :], scol[:, 24:25], laminit[:, l, 1:2], None, ALU.mult
                              ).then_inc(sem("col_ready"), 1)
            dve.wait_ge(sem("col_ready"), at("col_ready", l, 1))

        for l in range(DEPTH):
            def aux(r):
                return ps[:, 6 + r % 2, :]

            def mean_root(width, name, k):
                dve.wait_ge(sem(name + "sumsq"), at(name + "sumsq", l, k))
                dve.tensor_scalar(st[:, 3:6], st[:, 0:3], 1.0 / width, EPS, ALU.mult, ALU.add
                                  ).then_inc(sem(name + "meansq"), 1)
                dve.wait_ge(sem(name + "root"), at(name + "root", l, k))
                link(dve.reciprocal(st[:, 9:12], st[:, 6:9]))

            def norm_rows(which):
                mean_root(D, "", which + 1)
                for t in range(NT):
                    ins = dve.tensor_scalar(xn[:, t, :], x[:, t, :], st[:, 9 + t:10 + t], None, ALU.mult)
                ins.then_inc(sem("xn_done"), 1)

            def norm_cols(which, r0):
                for k in range(KD + 1):
                    if k < KD:
                        r = r0 + k
                        dve.wait_ge(sem("aux_ready"), at("aux_ready", l, r + 1))
                        if k >= 2:
                            dve.wait_ge(sem("hT_ready"), at("hT_ready", l, which * KD + k - 1))
                        dve.tensor_scalar(full[:, k % 2, 0:P], aux(r)[:, 0:P], scl[:, which, k, 0:1],
                                          shf[:, which, k, 0:1], ALU.mult, ALU.add).then_inc(sem("full_prompt"), 1)
                        dve.tensor_scalar(full[:, k % 2, P:T], aux(r)[:, P:T], scl[:, which, k, 1:2],
                                          shf[:, which, k, 1:2], ALU.mult, ALU.add).then_inc(sem("full_done"), 1)
                        dve.wait_ge(sem("full_done"), at("full_done", l, which * KD + k + 1))
                        dve.sem_inc(sem("aux_free"), 1)
                    if k:
                        j = k - 1
                        dve.wait_ge(sem("hT_hi"), at("hT_hi", l, which * KD + j + 1))
                        dve.tensor_tensor(hTl[:, j, :], full[:, j % 2, :], hTh[:, j, :].bitcast(F32), ALU.subtract
                                          ).then_inc(sem("hT_ready"), 1)

            def split_lo(out, hi_part, r, name, n, ready):
                dve.wait_ge(sem(name), at(name, l, n + 1))
                dve.tensor_tensor(out, aux(r)[:, 0:T], hi_part.bitcast(F32), ALU.subtract
                                  ).then_inc(sem("aux_free"), 1)
                dve.wait_ge(sem("aux_free"), at("aux_free", l, r + 1))
                dve.sem_inc(sem(ready), 1)

            norm_rows(0)
            if l == 0:
                for p in range(MOD_STATS, DENSE0[0]):
                    lo(p)
                dve.wait_ge(sem("rw_hi"), 1)
                dve.tensor_tensor(rwl[:, :, :], rw[:, :, :], rwh[:, :, :].bitcast(F32), ALU.subtract
                                  ).then_inc(sem("rw_ready"), 1)
            if l == 0:
                columns(0)
            norm_cols(0, R_NORM1)

            dve.wait_ge(sem("small_in"), at("small_in", l, 16 * 4))
            dve.wait_ge(sem("qkn_in"), 64 * (l + 1))
            link(dve.tensor_tensor(lamv[:, 0:4:2, :], lamv[:, 0:4:2, :], lamv[:, 1:4:2, :], ALU.mult))
            dve.tensor_reduce(lam[:, 0:2], lamv[:, 0:4:2, :], AX.X, ALU.add).then_inc(sem("lam_dot"), 1)
            for i in range(2):
                for t in range(2):
                    dve.tensor_tensor(rope[:, i, t, 0, :], rope0[:, t, 0, :],
                                      qkn[:, i, :, :].rearrange("p m d -> p (m d)"), ALU.mult)
                    for j in range(2):
                        ins = dve.tensor_tensor(
                            rope[:, i, t, 1, :].rearrange("p (a j c) -> p a j c", j=2, c=16)[:, :, j, :],
                            rope0[:, t, 1, :].rearrange("p (a j c) -> p a j c", j=2, c=16)[:, :, j, :],
                            qkn[:, i, :, :].rearrange("p m d -> p (m d)").rearrange(
                                "p (a j c) -> p a j c", j=2, c=16)[:, :, 1 - j, :], ALU.mult)
            ins.then_inc(sem("rope_ready"), 1)
            mean_root(W, "v_", 1)
            for t in range(NT):
                ins = dve.scalar_tensor_tensor(uv[:, t, W:2 * W], uv[:, t, W:2 * W], st[:, 9 + t:10 + t],
                                               anorm[:, :], ALU.mult, ALU.mult)
            ins.then_inc(sem("vn_done"), 1)
            for i in range(2):
                r = R_WS + i
                dve.wait_ge(sem("aux_ready"), at("aux_ready", l, r + 1))
                dve.tensor_copy(wsT[:, 4 * i:4 * i + 4, :], aux(r).rearrange("p (g n) -> p g n", g=4)
                                ).then_inc(sem("aux_free"), 1)
            for i in range(4):
                r = R_SV + i
                dve.wait_ge(sem("aux_ready"), at("aux_ready", l, r + 1))
                for j in range(2):
                    g = 2 * i + j
                    u = uv[:, :, g * 64:(g + 1) * 64]
                    ins = dve.scalar_tensor_tensor(u, aux(r)[:, j * 192:(j + 1) * 192].rearrange("p (t c) -> p t c", t=NT),
                                                   scol[:, 16 + g:17 + g], u, ALU.add, ALU.mult)
                ins.then_inc(sem("aux_free"), 1)
            dve.wait_ge(sem("aux_free"), at("aux_free", l, R_SV + 4))
            dve.sem_inc(sem("ya_tok"), 1)
            for i in range(4):
                split_lo(yaT[:, 1, i, :], yaT[:, 0, i, :], R_YA + i, "ya_hi", i, "ya_ready")
            for g in range(4):
                r = R_DFT + 3 * g
                dve.wait_ge(sem("aux_ready"), at("aux_ready", l, r + 1))
                if g:
                    dve.wait_ge(sem("aux_ready"), at("aux_ready", l, r))
                dve.tensor_copy(spec[:, :, P:T], aux(r).rearrange("p (s n) -> p s n", s=2)
                                ).then_inc(sem("aux_free"), 1)
                dve.wait_ge(sem("aux_ready"), at("aux_ready", l, r + 2))
                dve.tensor_copy(spec[:, :, 0:P], aux(r + 1)[:, 0:256].rearrange("p (s n) -> p s n", s=2)
                                ).then_inc(sem("aux_free"), 1)
                dve.wait_ge(sem("aux_free"), at("aux_free", l, r + 2))
                dve.sem_inc(sem("dft_copied"), 1)
                split_lo(ycT[:, 1, g, :], ycT[:, 0, g, :], r + 2, "yc_hi", g, "yc_ready")

            dve.wait_ge(sem("lam_exp"), at("lam_exp", l, 1))
            link(dve.tensor_tensor(lam[:, 4:5], lam[:, 3:4], lam[:, 2:3], ALU.subtract))
            dve.tensor_tensor(lam[:, 5:6], lam[:, 4:5], laminit[:, l, 0:1], ALU.subtract
                              ).then_inc(sem("lam_ready"), 1)
            dve.wait_ge(sem("rope_ready"), at("rope_ready", l, 1))
            tmp = ropetmp
            for s in range(2):
                three = slice(s * NT, (s + 1) * NT)
                for t in range(NT):
                    i = s * NT + t
                    dve.wait_ge(sem("qk_sumsq"), at("qk_sumsq", l, i + 1))
                    dve.tensor_reduce(qst[:, i, :], qsq[:, :].rearrange("p (n d) -> p n d", d=DQ), AX.X, ALU.add
                                      ).then_inc(sem("qk_summed"), 1)
                dve.wait_ge(sem("qk_summed"), at("qk_summed", l, (s + 1) * NT))
                dve.tensor_scalar(qst[:, three, :], qst[:, three, :], 1.0 / DQ, EPS, ALU.mult, ALU.add
                                  ).then_inc(sem("qk_meansq"), 1)
                dve.wait_ge(sem("qk_root"), at("qk_root", l, s + 1))
                link(dve.reciprocal(qst[:, three, :], qst[:, three, :]))
                dve.wait_ge(sem("evac_act"), at("evac_act", l, 5 + 2 * s))
                for t in range(NT):
                    i = s * NT + t
                    v = qk[:, :, s, t, :]
                    r4 = qst[:, i, :].rearrange("p (h m) -> p h m", m=MAPS).unsqueeze(3).to_broadcast([P, HEADS, MAPS, DQ])
                    v4 = v.rearrange("p h (m d) -> p h m d", m=MAPS)
                    link(dve.tensor_tensor(v4, v4, r4, ALU.mult))
                    if t == 0:
                        w = qkn[:, s, :, :].rearrange("p m d -> p (m d)").unsqueeze(1).to_broadcast([P, HEADS, P])
                        ins = dve.tensor_tensor(v, v, w, ALU.mult)
                    else:
                        for j in range(2):
                            src = v.rearrange("p h (a j c) -> p h a j c", j=2, c=16)[:, :, :, 1 - j, :]
                            dst = tmp[:, :, :].rearrange("p h (a j c) -> p h a j c", j=2, c=16)[:, :, :, j, :]
                            sn = rope[:, s, t - 1, 1, :].rearrange("p (a j c) -> p a j c", j=2, c=16)[:, :, j, :]
                            ins = dve.tensor_tensor(dst, src, sn.unsqueeze(1).to_broadcast([P, HEADS, 4, 16]), ALU.mult)
                        link(ins)
                        cos = rope[:, s, t - 1, 0, :].unsqueeze(1).to_broadcast([P, HEADS, P])
                        link(dve.tensor_tensor(v, v, cos, ALU.mult))
                        ins = dve.tensor_tensor(v, v, tmp[:, :, :], ALU.add)
                        if i < 2 * NT - 1:
                            link(ins)
            ins.then_inc(sem("qk_normed"), 1)

            merge_at = {(1, 2): 0, (3, 2): 1, (5, 2): 2, (7, 2): 3}

            def merge(n):
                u = FIRST_BR + 2 * n + 1
                base = 0 if u < FIRST_BR + 8 else 3 * (u % 2)
                half = n % 2
                m = merged[:, :, half * W:(half + 1) * W]
                dve.wait_ge(sem("pair_used"), use_end(l, u))
                if n < 2:
                    dve.tensor_tensor(m, ps[:, base:base + NT, :], gs[:, :, :], ALU.mult).then_inc(sem("evac_dve"), 1)
                    dve.wait_ge(sem("evac_dve"), at("evac_dve", l, n + 1))
                    dve.sem_inc(sem("merged_done"), 1)
                else:
                    dve.tensor_tensor(gs[:, :, :], ps[:, base:base + NT, :], gs[:, :, :], ALU.mult
                                      ).then_inc(sem("evac_dve"), 1)
                    dve.wait_ge(sem("evac_dve"), at("evac_dve", l, n + 1))
                    dve.tensor_tensor(m, m, gs[:, :, :], ALU.add).then_inc(sem("merged_done"), 1)

            dve.wait_ge(sem("lam_ready"), at("lam_ready", l, 1))
            for h in range(HEADS):
                dve.wait_ge(sem("qkT_acc"), at("qkT_acc", l, h + 1))
                dve.tensor_copy(kT[:, :], ps[:, 7, :]).then_inc(sem("kT_done"), 1)
                for i, t in enumerate((1, 0, 2)):
                    if t != 0:
                        dve.wait_ge(sem("score_acc"), at("score_acc", l, 2 * h + t))
                    if t == 0:
                        src = ps[:, 4:6, T:4 * P]
                    else:
                        b = 4 if t == 1 else 6
                        src = ps[:, b:b + 2, 0:T]
                    link(dve.tensor_reduce(mx[:, t, :], src, AX.X, ALU.max))
                    dve.tensor_scalar(nmx[:, t, :], mx[:, t, :], -DQ ** -0.5, None, ALU.mult
                                      ).then_inc(sem("score_max"), 1)
                for i, t in enumerate((1, 0, 2)):
                    dve.wait_ge(sem("exp_done"), at("exp_done", l, 3 * h + i + 1))
                    link(dve.reciprocal(er[:, t, :], es[:, t, :]))
                    link(dve.tensor_tensor(er[:, t, 1:2], er[:, t, 1:2], lam[:, 5:6], ALU.mult))
                    a = e0 if t == 0 else e12[:, t - 1, :, :]
                    link(dve.tensor_scalar(a[:, 0, :], a[:, 0, :], er[:, t, 0:1], None, ALU.mult))
                    dve.scalar_tensor_tensor(a[:, 0, :], a[:, 1, :], er[:, t, 1:2], a[:, 0, :], ALU.mult, ALU.add
                                             ).then_inc(sem("diff_done"), 1)
                if h % 2 == 1 and h < HEADS - 1:
                    merge(h // 2)
                dve.wait_ge(sem("o_acc"), at("o_acc", l, h + 1))
                dve.tensor_copy(qk[:, h, 0, :, :], ps[:, 4, 0:T].rearrange("p (t d) -> p t d", t=NT)
                                ).then_inc(sem("o_copied"), 1)
            merge(HEADS // 2 - 1)
            for t in range(NT):
                dve.wait_ge(sem("o_sq"), at("o_sq", l, t + 1))
                dve.tensor_reduce(qst[:, t, 0:8], o_sq[:, :].rearrange("p (h d) -> p h d", h=HEADS), AX.X, ALU.add
                                  ).then_inc(sem("o_summed"), 1)
            dve.wait_ge(sem("o_summed"), at("o_summed", l, NT))
            dve.tensor_scalar(qst[:, 0:3, 0:8], qst[:, 0:3, 0:8], 1.0 / P, EPS, ALU.mult, ALU.add
                              ).then_inc(sem("o_meansq"), 1)
            dve.wait_ge(sem("o_root"), at("o_root", l, 1))
            link(dve.reciprocal(qst[:, 0:3, 0:8], qst[:, 0:3, 0:8]))
            dve.wait_ge(sem("kv_out"), at("kv_out", l, 32))
            for t in range(NT):
                v = qk[:, :, 0, t, :]
                ins = dve.tensor_tensor(v, v, qst[:, t, 0:8].unsqueeze(2).to_broadcast([P, HEADS, P]), ALU.mult)
            ins.then_inc(sem("o_normed"), 1)
            for h in range(HEADS):
                r = R_YB + h
                dve.wait_ge(sem("yb_hi"), at("yb_hi", l, h + 1))
                dve.scalar_tensor_tensor(ybT[:, h, 1, :], aux(r)[:, 0:T], subc[:, 0:1], ybT[:, h, 0, :].bitcast(F32),
                                         ALU.mult, ALU.subtract).then_inc(sem("aux_free"), 1)
                dve.wait_ge(sem("aux_free"), at("aux_free", l, r + 1))
                dve.sem_inc(sem("yb_ready"), 1)
            merge(4)
            for k in range(4):
                split_lo(mT[:, 1, k, :], mT[:, 0, k, :], R_MERGED + k, "mT_hi", k, "mT_ready")
            merge(5)
            for k in range(4, KD):
                split_lo(mT[:, 1, k, :], mT[:, 0, k, :], R_MERGED + k, "mT_hi", k, "mT_ready")
            low_next = [MOD0[l]]

            def lo_upto(i):
                while low_next[0] < min(MOE0[l], MOD0[l] + i + 1):
                    lo(low_next[0])
                    low_next[0] += 1

            for half in range(2):
                u = len(USES) - 2 + half
                bank = 3 * (u % 2)
                c = slice(half * W, (half + 1) * W)
                dve.wait_ge(sem("pair_used"), use_end(l, u))
                for t in range(NT):
                    ins = dve.tensor_tensor(gs[:, t, :], ps[:, bank + t, :], gbc[:, 0, min(t, 1), c], ALU.mult)
                    if t == NT - 1:
                        ins.then_inc(sem("evac_dve"), 1)
                        dve.wait_ge(sem("evac_dve"), at("evac_dve", l, 7 + half))
                    else:
                        link(ins)
                    ins = dve.tensor_tensor(x[:, t, c], x[:, t, c], gs[:, t, :], ALU.add)
                    if half:
                        ins.then_inc(sem("x_mid"), 1)
                if not half:
                    link(ins)
            lo_upto(MOD_FIRST - 1)
            norm_rows(1)
            norm_cols(1, R_NORM2)
            lo_upto(MOD_FIRST + 1)
            dve.wait_ge(sem("score_done"), at("score_done", l, 1))

            steps = [0]

            def step(ins):
                link(ins)
                steps[0] += 1
                if steps[0] % 4 == 0:
                    lo_upto(low_next[0] - MOD0[l] + 1)

            sb, selv, gt, eq = rt[:, 0, 0:48], rt[:, 1, 0:48], rt[:, 2, :], rt[:, 3, :]
            rank, pair, grank, wgt, den = rt[:, 4, 0:48], rt[:, 5, 0:12], rt[:, 5, 16:28], rt[:, 6, 0:48], rt[:, 7, 0:6]
            link(dve.tensor_tensor(sb.rearrange("p (t e) -> p t e", t=NT), s_r[:, :, :],
                                   rb[:, :].unsqueeze(1).to_broadcast([P, NT, NE]), ALU.add))

            def ranks(vals, out, n):
                v = vals.rearrange("p (g i) -> p g i", i=EG)
                vi = v.unsqueeze(3).to_broadcast([P, n, EG, EG])
                vj = v.unsqueeze(2).to_broadcast([P, n, EG, EG])
                gv = gt[:, 0:n * EG * EG].rearrange("p (g i j) -> p g i j", i=EG, j=EG)
                ev = eq[:, 0:n * EG * EG].rearrange("p (g i j) -> p g i j", i=EG, j=EG)
                dve.tensor_tensor(gv, vj, vi, ALU.is_gt)
                step(dve.tensor_tensor(ev, vj, vi, ALU.is_equal))
                step(dve.tensor_tensor(ev, ev, rank_tri[:, :, :].unsqueeze(1).to_broadcast([P, n, EG, EG]), ALU.mult))
                step(dve.tensor_tensor(gv, gv, ev, ALU.add))
                step(dve.tensor_reduce(out.rearrange("p (g i) -> p g i", i=EG), gv, AX.X, ALU.add))

            ranks(sb, rank, 12)
            step(dve.tensor_scalar(selv, rank, 2.0, None, ALU.is_lt))
            step(dve.tensor_tensor(wgt, selv, sb, ALU.mult))
            step(dve.tensor_reduce(pair, wgt.rearrange("p (g i) -> p g i", i=EG), AX.X, ALU.add))
            ranks(pair, grank, NT)
            step(dve.tensor_scalar(grank, grank, 1.0, None, ALU.is_lt))
            m48 = mask[:, :, :].rearrange("p t e -> p (t e)")
            dve.tensor_tensor(m48.rearrange("p (g i) -> p g i", i=EG), selv.rearrange("p (g i) -> p g i", i=EG),
                              grank.unsqueeze(2).to_broadcast([P, 12, EG]), ALU.mult).then_inc(sem("mask_done"), 1)
            dve.wait_ge(sem("mask_done"), at("mask_done", l, 1))
            step(dve.tensor_tensor(wgt, s_r[:, :, :].rearrange("p t e -> p (t e)"), m48, ALU.mult))
            step(dve.tensor_reduce(den[:, 0:3], wgt.rearrange("p (t e) -> p t e", t=NT), AX.X, ALU.add))
            step(dve.reciprocal(den[:, 3:6], den[:, 0:3]))
            step(dve.tensor_tensor(gate[:, :, :], wgt.rearrange("p (t e) -> p t e", t=NT),
                                   den[:, 3:6].unsqueeze(2).to_broadcast([P, NT, NE]), ALU.mult))
            lo_upto(MOD_SLOTS)
            dve.wait_ge(sem("aux_ready"), at("aux_ready", l, R_SLOTS + 1))
            link(dve.scalar_tensor_tensor(slot[:, :, :].rearrange("p t e -> p (t e)"), aux(R_SLOTS)[:, 0:48], SLOT_BASE + 1.0, m48,
                                          ALU.add, ALU.mult))
            link(dve.tensor_scalar(slot[:, :, :], slot[:, :, :], -1.0, None, ALU.add))
            link(dve.tensor_reduce(cnt[:, 0:1], aux(R_SLOTS)[:, 48:64], AX.X, ALU.max))
            dve.tensor_scalar(flag[:, 0:1], cnt[:, 0:1], float(P - SLOT_BASE), None, ALU.is_gt).then_inc(sem("flag_ready"), 1)
            dve.sem_inc(sem("aux_free"), 1)
            dve.sem_inc(sem("slot_done"), 1)

            def expert_lo(e, q):
                if q % PAIRS_EXPERT in POOL_Q:
                    return
                dve.wait_ge(sem("hi_done"), used_at(l, e, q))
                dve.tensor_tensor(wxl[:, q % RING_MOE, :, :], raw[:, expert_chunk(l, 0, q // 2)[0], 2 * (q % 2):2 * (q % 2) + 2, :],
                                  wxh[:, q % RING_MOE, :, :].bitcast(F32), ALU.subtract).then_inc(sem("lo_dve"), 1)

            def make_pick(e, pair, odd):
                for t in range(NT):
                    ins = dve.tensor_scalar(pick[:, t, pair, odd * P:(odd + 1) * P], iota[:, :],
                                            slot[:, t, bass.ds(e, 1)], None, ALU.is_equal)
                ins.then_inc(sem("pick_ready"), 1)

            def gathered(count, half, bank):
                dve.wait_ge(sem("xe_hi"), count)
                k = slice(4 * half, 4 * half + 4)
                dve.tensor_tensor(xeT[:, 1, k, :], ps[:, bank:bank + 2, :].rearrange("p b (k n) -> p (b k) n", k=2),
                                  xeT[:, 0, k, :].bitcast(F32), ALU.subtract).then_inc(sem("xe_ready"), 1)

            def out_lo(e):
                dve.wait_ge(sem("out_hi"), at("out_hi", l, 1) + e)
                dve.tensor_tensor(oe[:, 1, :].rearrange("p (b n) -> p b n", b=2), ps[:, 4:6, :],
                                  oe[:, 0, :].bitcast(F32).rearrange("p (b n) -> p b n", b=2), ALU.subtract
                                  ).then_inc(sem("out_ready"), 1)

            def combine(e, c):
                t, half = c // 2, c % 2
                dst = y[:, t, half * W:(half + 1) * W]
                dve.wait_ge(sem("comb_acc"), at("comb_acc", l, c + 1) + e * 6)
                dve.scalar_tensor_tensor(dst, ps[:, 6 + c % 2, :], gate[:, t, bass.ds(e, 1)], dst, ALU.mult, ALU.add
                                         ).then_inc(sem("comb_done"), 1)

            def expert(e, odd, pair, first=False, last_pair=False, last_one=False):
                if not odd and not last_pair:
                    if not first:
                        dve.wait_ge(sem("PT_acc"), at("PT_acc", l, 0) + e)
                    make_pick(e + 2, 1 - pair, 0)
                    make_pick(e + 3, 1 - pair, 1)
                expert_lo(e, 3)
                expert_lo(e, 4)
                for c in range(5):
                    expert_lo(e, 5 + c)
                    if not first:
                        combine(e - 1, c)
                dve.wait_ge(sem("silu_done"), at("silu_done", l, 1) + e)
                dve.wait_ge(sem("pair_used"), used_at(l, e, 7))
                dve.tensor_tensor(ae[:, :], ps[:, 3, :], sg[:, :], ALU.mult).then_inc(sem("a_done"), 1)
                if not first:
                    combine(e - 1, 5)
                expert_lo(e, 10)
                dve.wait_ge(sem("eT_hi"), at("eT_hi", l, 1) + e)
                dve.tensor_tensor(eaT[:, 1, :, :], ps[:, 4, :].rearrange("p (k n) -> p k n", k=4),
                                  eaT[:, 0, :, :].bitcast(F32), ALU.subtract).then_inc(sem("eT_ready"), 1)
                expert_lo(e, 11)
                if odd and not last_pair:
                    gathered(at("xe_hi", l, 2) + e, 0, 0)
                    gathered(at("xe_hi", l, 3) + e, 1, 2)
                if not last_one:
                    for q in range(12, 15):
                        expert_lo(e, q)
                out_lo(e)

            dve.wait_ge(sem("flag_ready"), at("flag_ready", l, 1))
            dve.wait_ge(sem("slot_done"), at("slot_done", l, 1))
            make_pick(0, 0, 0)
            make_pick(1, 0, 1)
            lo_upto(MOD_GATHER + 1)
            gathered(at("xe_hi", l, 1), 0, 0)
            lo_upto(MOD_GATHER + MOD_BETWEEN + 1)
            gathered(at("xe_hi", l, 2), 1, 0)
            lo_upto(MOE0[l])
            if l + 1 < DEPTH:
                columns(l + 1)
            for q in range(3):
                expert_lo(0, q)
            dve.wait_ge(sem("y_zero"), at("y_zero", l, 1))
            expert_loop(dve, expert)
            for c in range(6):
                combine(NE - 1, c)
            dve.wait_ge(sem("comb_done"), at("comb_done", l, 6 * NE))

            def turn(e, b):
                over_dve = sem(f"over_dve{l}")

                def wait_act(k):
                    dve.wait_ge(sem(f"over_act{l}"), over_at("act", e, b, k))

                def wait_pe(k):
                    dve.wait_ge(sem(f"over_pe{l}"), over_at("pe", e, b, k))

                def chunk(i):
                    wait_act(OVER_ACT[f"c{i}"])
                    dve.tensor_tensor(wl[:, 0:2, :, :].rearrange("p r i n -> p (r i) n"), raw[:, 0, :, :],
                                      wh[:, 0:2, :, :].rearrange("p r i n -> p (r i) n").bitcast(F32), ALU.subtract
                                      ).then_inc(over_dve, 1)

                dve.tensor_scalar(cnt[:, 2:5], slot[:, :, bass.ds(e, 1)].rearrange("p t a -> p (t a)"),
                                  float(-P * b), None, ALU.add).then_inc(sem(f"over_col{l}"), 1)
                dve.tensor_copy(cnt[:, 5:8], gate[:, :, bass.ds(e, 1)].rearrange("p t a -> p (t a)")
                                ).then_inc(sem(f"over_col{l}"), 1)
                dve.wait_ge(sem(f"over_col{l}"), e * 4 + 2 * b)
                for t in range(NT):
                    ins = dve.tensor_scalar(pick1[:, t, :], iota[:, :], cnt[:, 2 + t:3 + t], None, ALU.is_equal)
                ins.then_inc(over_dve, 1)
                wait_act(OVER_ACT["x_hi"])
                dve.tensor_tensor(xeT1[:, 1, :, :], ps[:, 0:2, :].rearrange("p b (k n) -> p (b k) n", k=4),
                                  xeT1[:, 0, :, :].bitcast(F32), ALU.subtract).then_inc(over_dve, 1)
                dve.tensor_copy(pickT[:, 0, :, :], ps[:, 6, 0:T].rearrange("p (t n) -> p t n", t=NT)
                                ).then_inc(over_dve, 1)
                for i in range(4):
                    chunk(i)
                wait_act(OVER_ACT["silu"])
                wait_pe(OVER_PE["c3"])
                dve.tensor_tensor(ae[:, :], ps[:, 3, :], sg[:, :], ALU.mult).then_inc(over_dve, 1)
                wait_act(OVER_ACT["a_hi"])
                dve.tensor_tensor(eaT[:, 1, :, :], ps[:, 7, :].rearrange("p (k n) -> p k n", k=4),
                                  eaT[:, 0, :, :].bitcast(F32), ALU.subtract).then_inc(over_dve, 1)
                chunk(4)
                chunk(5)
                wait_act(OVER_ACT["out_hi"])
                dve.tensor_tensor(oe[:, 1, :].rearrange("p (b n) -> p b n", b=2), ps[:, 4:6, :],
                                  oe[:, 0, :].bitcast(F32).rearrange("p (b n) -> p b n", b=2), ALU.subtract
                                  ).then_inc(over_dve, 1)
                for c in range(6):
                    t, half = c // 2, c % 2
                    dst = y[:, t, half * W:(half + 1) * W]
                    wait_pe(OVER_PE["part"] + c)
                    dve.scalar_tensor_tensor(dst, ps[:, 6 + c % 2, :], cnt[:, 5 + t:6 + t], dst, ALU.mult, ALU.add
                                             ).then_inc(over_dve, 1)
                dve.wait_ge(over_dve, over_at("dve", e, b, OVER_STEPS["dve"]))

            second_pass(dve, l, turn)
            for t in range(NT):
                link(dve.tensor_tensor(y[:, t, :], y[:, t, :], gbc[:, 1, min(t, 1), :], ALU.mult))
                dve.tensor_tensor(x[:, t, :], x[:, t, :], y[:, t, :], ALU.add).then_inc(sem("x_ready"), 1)

    junk_n = [0]
    COLS_IN = [16 * 5]
    for l in range(DEPTH):
        COLS_IN.append(COLS_IN[-1] + 16 * (6 if l + 1 < DEPTH else 1))
    o_sq = place("o_sq", [P, D], F32, r_z)
    ropetmp = place("ropetmp", [P, HEADS, P], F32, r_z)
    A = slice(None)

    def first_loads():
        return [
            (ident[:, :], io["t_ident"]),
            (crow[0:8, :], io["c"].rearrange("a (k p) -> (a k) p", p=P)),
            (crow[8:16, :], io["c_ctx"].rearrange("(k p) -> k p", p=P)),
        ]

    def const_loads():
        return [
            (tri[:, :, :], io["t_tri"]), (iota[:, :], io["t_iota"]),
            (rank_tri[:, :, :], io["t_rank_tri"]), (sel2[:, :], io["t_sel2"]), (selb[:, :, :], io["t_selb"]),
            (laminit[:, :, :], io["t_laminit"]),
            (rw[:, :, :], io["router_w"].rearrange("(k p) e -> p k e", p=P)),
            (rb[:, :], io["router_b"].rearrange("(a e) -> a e", a=1).broadcast_to([P, NE])),
        ]

    N_CONST = len(const_loads())
    with nc.Block() as block:
        block.sync(sync_program)
        block.tensor(tensor_program)
        block.scalar(scalar_program)
        block.gpsimd(gpsimd_program)
        block.vector(vector_program)


_INS = ['x_prompt', 'x_sample', 'cache_k', 'cache_v', 'c', 'c_ctx', 'w_mod', 'b_mod', 'norm1_w', 'norm2_w', 'w_in',
        'a_norm_w', 'a_w_s', 'a_b_s', 'q_norm_w', 'k_norm_w', 'lambda_qk', 'subln_w', 'w_br_a', 'w_br_b', 'w_br_c',
        'w_out', 'router_w', 'router_b', 'w_e_gate', 'w_e_up', 'w_e_down']
_OUTS = [("y_prompt", (1, 128, 1024)), ("y_sample", (1, 256, 1024)), ("new_k", (1, DEPTH, 128, 8, 128)),
         ("new_v", (1, DEPTH, 128, 8, 128))]


def tables():
    import numpy as np

    f = np.float32
    i = np.arange(P)
    t = {"t_ident": np.eye(P, dtype=f)}
    t["t_tri"] = np.stack([(i[:, None] < i[None, :]), np.ones((P, P), bool)], 1).astype(f)
    t["t_iota"] = np.broadcast_to(np.arange(P, dtype=f), (P, P)).copy()
    j = np.arange(EG)
    t["t_rank_tri"] = np.broadcast_to((j[None, :] < j[:, None]).astype(f), (P, EG, EG)).copy()
    rows = np.array([[1, 0], [0, 1], [1, 0], [0, 1], [1, 1]], f)
    t["t_sel2"] = rows
    t["t_selb"] = np.repeat(rows[:, :, None], P, 2)
    n = np.arange(2 * P)
    freq = (np.float32(10000.0) ** (-np.arange(16, dtype=f) / f(16))).astype(f)
    ang = np.stack([(n // 64).astype(f)[:, None] * freq, (n % 64).astype(f)[:, None] * freq], 1)
    cos, sin = np.cos(ang), np.sin(ang)
    c = np.stack([cos, cos], 2).reshape(2 * P, 64)
    s = np.stack([-sin, sin], 2).reshape(2 * P, 64)
    cs = np.stack([np.tile(c, (1, 2)), np.tile(s, (1, 2))], 1).astype(f)
    t["t_rope"] = cs.reshape(2, P, 2, P).transpose(1, 0, 2, 3).copy()
    t["t_laminit"] = np.broadcast_to(np.array([[v, 1 - v] for v in LAM_INIT], f), (P, DEPTH, 2)).copy()

    def dft(length):
        a = 2 * np.pi * (np.outer(np.arange(length), np.arange(length)) % length) / length
        return np.cos(a) / np.sqrt(length), -np.sin(a) / np.sqrt(length)

    c, s = dft(256)
    t["t_dft_lat"] = np.stack([c, s], 1).reshape(2, P, 2, 256).transpose(1, 0, 2, 3).astype(f).copy()
    c, s = dft(P)
    t["t_dft_pr"] = np.stack([c, s], 1).astype(f)
    t["t_dft_ch"] = np.stack([c, -s], 1).astype(f)
    return t


def kernel(**inputs):
    import numpy as np
    import concourse.bacc as bacc
    from concourse.bass_utils import run_bass_kernel_spmd as run

    nc = bacc.Bacc("TRN2", target_bir_lowering=False, num_devices=1)
    arrays, io = {}, {}
    for name in _INS:
        arrays[name] = np.ascontiguousarray(inputs[name])
    arrays.update(tables())
    for name, a in arrays.items():
        io[name] = nc.dram_tensor(name, a.shape, F32, kind="ExternalInput").ap()
    for name, shape in _OUTS:
        io[name] = nc.dram_tensor(name, shape, F32, kind="ExternalOutput").ap()
    build(nc, io)
    r = run(nc, [arrays], core_ids=[0])
    return tuple(r.results[0][name] for name, _ in _OUTS)
```
